# Optimizing a Trainium2 kernel written in Bass

```python
import math
import jax, jax.numpy as jnp
from jax import lax
import numpy as np

"""One inference step of a hybrid diffusion / flow-matching trunk (DEPTH interleaved layers).

Layer i uses token mixer (i mod 2): even layers = bidirectional multi-scale retention
(RetNet, chunkwise-recurrent form), odd layers = multi-head latent attention (DeepSeek-V3
style, low-rank KV + decoupled rotary key with 2-D axial rotary on latent tokens). Every
layer is followed by an expert-choice routed SwiGLU mixture (16 experts, capacity factor 2).
Every sub-layer: sandwich RMSNorm + adaLN (shift/scale/gate from SiLU(cond) @ W + b), cond = c
for latent tokens, cond = c_ctx for context tokens.

Inputs:
  x_prompt        (BATCH, SEQ, D_MODEL)          context tokens of new requests (group i)
  x_sample        (DEC_BATCH, DEC_SEQ, D_MODEL)  noisy latent tokens (group ii), grid width GRID_W
  state_ret_fwd   (DEC_BATCH, N_RET_LAYERS, RET_HEADS, RET_DK, RET_DV)  final forward context-scan state
  state_ret_bwd   (DEC_BATCH, N_RET_LAYERS, RET_HEADS, RET_DK, RET_DV)  final backward context-scan state
  cache_mla_ckv   (DEC_BATCH, N_MLA_LAYERS, PAST_LEN, MLA_KV_LORA)      normalised compressed context KV
  cache_mla_krope (DEC_BATCH, N_MLA_LAYERS, PAST_LEN, MLA_ROPE)         context decoupled rotary key (no position)
  c               (DEC_BATCH, D_MODEL)           conditioning vectors of the latent requests
  c_ctx           (D_MODEL,)                     learned context conditioning vector
  followed by the weights.
Output tuple:
  (y_prompt (BATCH, SEQ, D_MODEL),
   y_sample (DEC_BATCH, DEC_SEQ, D_MODEL),
   new_state_ret_fwd (BATCH, N_RET_LAYERS, RET_HEADS, RET_DK, RET_DV),
   new_state_ret_bwd (BATCH, N_RET_LAYERS, RET_HEADS, RET_DK, RET_DV),
   new_cache_mla_ckv (BATCH, N_MLA_LAYERS, SEQ, MLA_KV_LORA),
   new_cache_mla_krope (BATCH, N_MLA_LAYERS, SEQ, MLA_ROPE))
"""

D_MODEL = 1024
BATCH = 1
SEQ = 128
DEPTH = 2
DEC_BATCH = 1
DEC_SEQ = 512
PAST_LEN = 128

GRID_W = 64
N_MIXERS = 2
N_RET_LAYERS = (DEPTH + 1) // 2
N_MLA_LAYERS = DEPTH // 2
RET_HEADS = 4
RET_DK = D_MODEL // RET_HEADS
RET_DV = 2 * RET_DK
RET_QK_WIDTH = RET_HEADS * RET_DK
RET_V_WIDTH = RET_HEADS * RET_DV
RET_CHUNK = 128
MLA_HEADS = 8
MLA_NOPE = 128
MLA_ROPE = 64
MLA_V = 128
MLA_Q_LORA = 384
MLA_KV_LORA = 256
ROPE_BASE = 10000.0
Q_BLOCK = 128
N_EXPERTS = 16
EC_CAPACITY_FACTOR = 2
EXPERT_FF = 1024
NORM_EPS = 1e-6

kernel_name = "hybrid_retention_mla_ec_diffusion_step"

def rms_norm(x, gain):
    xf = x.astype(jnp.float32)
    y = xf * lax.rsqrt(jnp.mean(xf * xf, axis=-1, keepdims=True) + NORM_EPS)
    return (y * gain.astype(jnp.float32)).astype(x.dtype)

def head_group_norm(y):
    yf = y.astype(jnp.float32)
    mu = jnp.mean(yf, axis=-1, keepdims=True)
    var = jnp.mean(jnp.square(yf - mu), axis=-1, keepdims=True)
    return ((yf - mu) * lax.rsqrt(var + NORM_EPS)).astype(y.dtype)

def adaln_mod(cond, w, b):
    m = jax.nn.silu(cond) @ w + b
    m = m.reshape(m.shape[0], 1, 6, D_MODEL)
    return tuple(m[:, :, j] for j in range(6))

def axial_rope_tables(n_tokens):
    rows = n_tokens // GRID_W
    row = jnp.repeat(jnp.arange(rows, dtype=jnp.float32), GRID_W)
    col = jnp.tile(jnp.arange(GRID_W, dtype=jnp.float32), rows)
    half = MLA_ROPE // 2
    inv = 1.0 / (ROPE_BASE ** (jnp.arange(0, half, 2, dtype=jnp.float32) / half))
    ar = row[:, None] * inv
    ac = col[:, None] * inv
    ang = jnp.concatenate([ar, ar, ac, ac], axis=-1)
    return jnp.cos(ang), jnp.sin(ang)

def apply_axial_rope(x, cos, sin):
    x1, x2, x3, x4 = jnp.split(x, 4, axis=-1)
    rot = jnp.concatenate([-x2, x1, -x4, x3], axis=-1)
    return (x * cos + rot * sin).astype(x.dtype)

def chunk_retention(q, k, v, log_gamma, s0, strict):
    b, n, h, dk = q.shape
    dv = v.shape[-1]
    nc = n // RET_CHUNK
    dt = q.dtype
    pos = jnp.arange(RET_CHUNK, dtype=jnp.float32)
    diff = pos[:, None] - pos[None, :]
    mask = (diff > 0) if strict else (diff >= 0)
    lg = log_gamma[:, None, None]
    inner_decay = jnp.exp(jnp.where(mask[None], diff[None] * lg, -jnp.inf)).astype(dt)
    cross_decay = jnp.exp((pos + 1.0)[:, None] * log_gamma[None, :]).astype(dt)
    state_decay = jnp.exp((RET_CHUNK - 1.0 - pos)[:, None] * log_gamma[None, :]).astype(dt)
    chunk_decay = jnp.exp(RET_CHUNK * log_gamma).astype(dt)

    def to_chunks(t):
        return jnp.swapaxes(t.reshape(b, nc, RET_CHUNK, h, t.shape[-1]), 0, 1)

    def step(s, qkv):
        qc, kc, vc = qkv
        scores = jnp.einsum('bihd,bjhd->bhij', qc, kc) * inner_decay
        y = (jnp.einsum('bhij,bjhe->bihe', scores, vc)
             + jnp.einsum('bihd,bhde->bihe', qc, s) * cross_decay[None, :, :, None])
        s = (s * chunk_decay[None, :, None, None]
             + jnp.einsum('bjhd,bjhe->bhde', kc * state_decay[None, :, :, None], vc))
        return s, y

    s_final, ys = lax.scan(step, s0, (to_chunks(q), to_chunks(k), to_chunks(v)))
    return jnp.swapaxes(ys, 0, 1).reshape(b, n, h, dv), s_final

def retention_mixer(h, s_fwd0, s_bwd0, w_in, decay_fwd, decay_bwd, w_out):
    b, n, _ = h.shape
    q, k, v, g = jnp.split(h @ w_in, [RET_QK_WIDTH, 2 * RET_QK_WIDTH, 2 * RET_QK_WIDTH + RET_V_WIDTH], axis=-1)
    q = q.reshape(b, n, RET_HEADS, RET_DK)
    k = k.reshape(b, n, RET_HEADS, RET_DK) * (RET_DK ** -0.5)
    v = v.reshape(b, n, RET_HEADS, RET_DV)
    lg_f = jax.nn.log_sigmoid(decay_fwd.astype(jnp.float32))
    lg_b = jax.nn.log_sigmoid(decay_bwd.astype(jnp.float32))
    y_f, s_f = chunk_retention(q, k, v, lg_f, s_fwd0, False)
    flip = lambda t: jnp.flip(t, axis=1)
    y_b, s_b = chunk_retention(flip(q), flip(k), flip(v), lg_b, s_bwd0, True)
    y = head_group_norm(y_f + flip(y_b)).reshape(b, n, RET_V_WIDTH)
    return (jax.nn.silu(g) * y) @ w_out, s_f, s_b

def mla_project(h, w_in, q_norm, kv_norm, w_q_b):
    b, n, _ = h.shape
    q_lat, kv_lat, k_rope = jnp.split(h @ w_in, [MLA_Q_LORA, MLA_Q_LORA + MLA_KV_LORA], axis=-1)
    q = (rms_norm(q_lat, q_norm) @ w_q_b).reshape(b, n, MLA_HEADS, MLA_NOPE + MLA_ROPE)
    return q[..., :MLA_NOPE], q[..., MLA_NOPE:], rms_norm(kv_lat, kv_norm), k_rope

def mla_expand(kv_lat, w_kv_b):
    b, n, _ = kv_lat.shape
    kv = (kv_lat @ w_kv_b).reshape(b, n, MLA_HEADS, MLA_NOPE + MLA_V)
    return kv[..., :MLA_NOPE], kv[..., MLA_NOPE:]

def blocked_attention(q_nope, q_rope, k_nope, k_rope, v):
    b, nq, h, _ = q_nope.shape
    nb = nq // Q_BLOCK
    scale = 1.0 / math.sqrt(MLA_NOPE + MLA_ROPE)

    def to_blocks(t):
        return jnp.swapaxes(t.reshape(b, nb, Q_BLOCK, *t.shape[2:]), 0, 1)

    def one_block(qs):
        qn, qr = qs
        s = jnp.einsum('bqhd,bkhd->bhqk', qn, k_nope) + jnp.einsum('bqhd,bkd->bhqk', qr, k_rope)
        p = jax.nn.softmax(s.astype(jnp.float32) * scale, axis=-1).astype(v.dtype)
        return jnp.einsum('bhqk,bkhe->bqhe', p, v)

    out = lax.map(one_block, (to_blocks(q_nope), to_blocks(q_rope)))
    return jnp.swapaxes(out, 0, 1).reshape(b, nq, h, MLA_V)

def mla_context(h, w_in, q_norm, kv_norm, w_q_b, w_kv_b, w_out):
    b, n, _ = h.shape
    q_nope, q_rope, kv_lat, k_rope = mla_project(h, w_in, q_norm, kv_norm, w_q_b)
    k_nope, v = mla_expand(kv_lat, w_kv_b)
    o = blocked_attention(q_nope, q_rope, k_nope, k_rope, v)
    return o.reshape(b, n, MLA_HEADS * MLA_V) @ w_out, kv_lat, k_rope

def mla_latent(h, ckv_ctx, krope_ctx, cos, sin, w_in, q_norm, kv_norm, w_q_b, w_kv_b, w_out):
    b, n, _ = h.shape
    q_nope, q_rope, kv_lat, k_rope = mla_project(h, w_in, q_norm, kv_norm, w_q_b)
    q_rope = apply_axial_rope(q_rope, cos[None, :, None, :], sin[None, :, None, :])
    k_rope = apply_axial_rope(k_rope, cos[None], sin[None])
    k_nope_l, v_l = mla_expand(kv_lat, w_kv_b)
    k_nope_c, v_c = mla_expand(ckv_ctx, w_kv_b)
    k_nope = jnp.concatenate([k_nope_c, k_nope_l], axis=1)
    k_rope_all = jnp.concatenate([krope_ctx, k_rope], axis=1)
    v = jnp.concatenate([v_c, v_l], axis=1)
    o = blocked_attention(q_nope, q_rope, k_nope, k_rope_all, v)
    return o.reshape(b, n, MLA_HEADS * MLA_V) @ w_out

def expert_choice_ffn(h, w_router, w_gate, w_up, w_down):
    b, n, d = h.shape
    cap = EC_CAPACITY_FACTOR * n // N_EXPERTS
    affinity = jax.nn.softmax((h @ w_router).astype(jnp.float32), axis=-1)
    gate, idx = lax.top_k(jnp.swapaxes(affinity, 1, 2), cap)
    xe = jax.vmap(lambda hb, ib: hb[ib])(h, idx)
    a = jnp.einsum('becd,edf->becf', xe, w_gate)
    u = jnp.einsum('becd,edf->becf', xe, w_up)
    ye = jnp.einsum('becf,efd->becd', jax.nn.silu(a) * u, w_down) * gate[..., None].astype(h.dtype)
    return jax.vmap(lambda yb, ib: jnp.zeros((n, d), yb.dtype).at[ib.reshape(-1)].add(yb.reshape(-1, d)))(ye, idx)

def setup_inputs(seed: int = 0) -> dict:
    key = jax.random.key(seed)
    ks = jax.random.split(key, 26)

    def nrm(k, shape, scale):
        return jax.random.normal(k, shape, jnp.float32) * scale

    D = D_MODEL
    gam = 1.0 - 2.0 ** (-5.0 - jnp.arange(RET_HEADS, dtype=jnp.float32))
    decay_base = jnp.log(gam / (1.0 - gam))
    ret_in_width = 2 * RET_QK_WIDTH + 2 * RET_V_WIDTH
    return {
        "x_prompt": nrm(ks[0], (BATCH, SEQ, D), 1.0),
        "x_sample": nrm(ks[1], (DEC_BATCH, DEC_SEQ, D), 1.0),
        "state_ret_fwd": nrm(ks[2], (DEC_BATCH, N_RET_LAYERS, RET_HEADS, RET_DK, RET_DV), 0.5),
        "state_ret_bwd": nrm(ks[3], (DEC_BATCH, N_RET_LAYERS, RET_HEADS, RET_DK, RET_DV), 0.5),
        "cache_mla_ckv": nrm(ks[4], (DEC_BATCH, N_MLA_LAYERS, PAST_LEN, MLA_KV_LORA), 1.0),
        "cache_mla_krope": nrm(ks[5], (DEC_BATCH, N_MLA_LAYERS, PAST_LEN, MLA_ROPE), 1.0),
        "c": nrm(ks[6], (DEC_BATCH, D), 1.0),
        "c_ctx": nrm(ks[7], (D,), 1.0),
        "ada_w": nrm(ks[8], (DEPTH, D, 6 * D), 0.5 * D ** -0.5),
        "ada_b": nrm(ks[9], (DEPTH, 6 * D), 0.02),
        "norm_pre": 1.0 + nrm(ks[10], (DEPTH, 2, D), 0.02),
        "norm_post": 1.0 + nrm(ks[11], (DEPTH, 2, D), 0.02),
        "ret_w_in": nrm(ks[12], (N_RET_LAYERS, D, ret_in_width), D ** -0.5),
        "ret_decay_fwd": decay_base[None, :] + nrm(ks[13], (N_RET_LAYERS, RET_HEADS), 0.1),
        "ret_decay_bwd": decay_base[None, :] + nrm(ks[14], (N_RET_LAYERS, RET_HEADS), 0.1),
        "ret_w_out": nrm(ks[15], (N_RET_LAYERS, RET_V_WIDTH, D), RET_V_WIDTH ** -0.5),
        "mla_w_in": nrm(ks[16], (N_MLA_LAYERS, D, MLA_Q_LORA + MLA_KV_LORA + MLA_ROPE), D ** -0.5),
        "mla_q_norm": 1.0 + nrm(ks[17], (N_MLA_LAYERS, MLA_Q_LORA), 0.02),
        "mla_kv_norm": 1.0 + nrm(ks[18], (N_MLA_LAYERS, MLA_KV_LORA), 0.02),
        "mla_w_q_b": nrm(ks[19], (N_MLA_LAYERS, MLA_Q_LORA, MLA_HEADS * (MLA_NOPE + MLA_ROPE)), MLA_Q_LORA ** -0.5),
        "mla_w_kv_b": nrm(ks[20], (N_MLA_LAYERS, MLA_KV_LORA, MLA_HEADS * (MLA_NOPE + MLA_V)), MLA_KV_LORA ** -0.5),
        "mla_w_out": nrm(ks[21], (N_MLA_LAYERS, MLA_HEADS * MLA_V, D), (MLA_HEADS * MLA_V) ** -0.5),
        "moe_w_router": nrm(ks[22], (DEPTH, D, N_EXPERTS), D ** -0.5),
        "moe_w_gate": nrm(ks[23], (DEPTH, N_EXPERTS, D, EXPERT_FF), D ** -0.5),
        "moe_w_up": nrm(ks[24], (DEPTH, N_EXPERTS, D, EXPERT_FF), D ** -0.5),
        "moe_w_down": nrm(ks[25], (DEPTH, N_EXPERTS, EXPERT_FF, D), EXPERT_FF ** -0.5),
    }

def reference(x_prompt, x_sample, state_ret_fwd, state_ret_bwd, cache_mla_ckv, cache_mla_krope, c, c_ctx,
              ada_w, ada_b, norm_pre, norm_post, ret_w_in, ret_decay_fwd, ret_decay_bwd, ret_w_out,
              mla_w_in, mla_q_norm, mla_kv_norm, mla_w_q_b, mla_w_kv_b, mla_w_out,
              moe_w_router, moe_w_gate, moe_w_up, moe_w_down):
    cos, sin = axial_rope_tables(x_sample.shape[1])
    xp, xs = x_prompt, x_sample
    bp = xp.shape[0]
    new_fwd, new_bwd, new_ckv, new_krope = [], [], [], []
    for i in range(DEPTH):
        sh1_p, sc1_p, g1_p, sh2_p, sc2_p, g2_p = adaln_mod(c_ctx[None, :], ada_w[i], ada_b[i])
        sh1_s, sc1_s, g1_s, sh2_s, sc2_s, g2_s = adaln_mod(c, ada_w[i], ada_b[i])
        hp = rms_norm(xp, norm_pre[i, 0]) * (1.0 + sc1_p) + sh1_p
        hs = rms_norm(xs, norm_pre[i, 0]) * (1.0 + sc1_s) + sh1_s
        if i % N_MIXERS == 0:
            r = i // N_MIXERS
            zero_state = jnp.zeros((bp, RET_HEADS, RET_DK, RET_DV), xp.dtype)
            yp, s_f, s_b = retention_mixer(hp, zero_state, zero_state, ret_w_in[r],
                                           ret_decay_fwd[r], ret_decay_bwd[r], ret_w_out[r])
            ys = retention_mixer(hs, state_ret_fwd[:, r], state_ret_bwd[:, r], ret_w_in[r],
                                 ret_decay_fwd[r], ret_decay_bwd[r], ret_w_out[r])[0]
            new_fwd.append(s_f)
            new_bwd.append(s_b)
        else:
            m = i // N_MIXERS
            yp, ckv, krope = mla_context(hp, mla_w_in[m], mla_q_norm[m], mla_kv_norm[m],
                                         mla_w_q_b[m], mla_w_kv_b[m], mla_w_out[m])
            ys = mla_latent(hs, cache_mla_ckv[:, m], cache_mla_krope[:, m], cos, sin, mla_w_in[m],
                            mla_q_norm[m], mla_kv_norm[m], mla_w_q_b[m], mla_w_kv_b[m], mla_w_out[m])
            new_ckv.append(ckv)
            new_krope.append(krope)
        xp = xp + rms_norm(yp, norm_post[i, 0]) * g1_p
        xs = xs + rms_norm(ys, norm_post[i, 0]) * g1_s
        hp = rms_norm(xp, norm_pre[i, 1]) * (1.0 + sc2_p) + sh2_p
        hs = rms_norm(xs, norm_pre[i, 1]) * (1.0 + sc2_s) + sh2_s
        fp = expert_choice_ffn(hp, moe_w_router[i], moe_w_gate[i], moe_w_up[i], moe_w_down[i])
        fs = expert_choice_ffn(hs, moe_w_router[i], moe_w_gate[i], moe_w_up[i], moe_w_down[i])
        xp = xp + rms_norm(fp, norm_post[i, 1]) * g2_p
        xs = xs + rms_norm(fs, norm_post[i, 1]) * g2_s
    return (xp, xs, jnp.stack(new_fwd, axis=1), jnp.stack(new_bwd, axis=1),
            jnp.stack(new_ckv, axis=1), jnp.stack(new_krope, axis=1))


_drawn_inputs = setup_inputs


def setup_inputs(seed=0):
    import zlib

    import numpy as np

    out = dict(_drawn_inputs(seed))
    spreads = {}
    factors = {'mla_q_norm': 3.282, 'mla_kv_norm': 8.237, 'cache_mla_ckv': 8.0, 'cache_mla_krope': 8.0}
    for name, (base, spread) in spreads.items():
        noise = np.random.default_rng([zlib.crc32(name.encode()), seed]).standard_normal(out[name].shape)
        drawn = base * np.exp(spread * noise) if base else spread * noise
        out[name] = __import__('jax').numpy.asarray(drawn.astype(out[name].dtype))
    for name, factor in factors.items():
        out[name] = (out[name] * factor).astype(out[name].dtype)
    return out
```

```python
from contextlib import ExitStack

import concourse.bass as bass
from concourse import mybir

F32 = mybir.dt.float32
ALU = mybir.AluOpType
ACT = mybir.ActivationFunctionType
AX = mybir.AxisListType.X

P = 128
D = 1024
KD = D // P
NLAT = 4
NT = 5
LAT = NLAT * P
TOK = NT * P
DEPTH = 2
ADA_CHUNKS = 12
HALF = 512
SLOT = 4096
HEADS = 4
DK, DV = 256, 512
NE = 16
PAIRS = NE // 2
CAP = 64
CAPP = 16
ROWS = CAP + CAPP
MH = 8
QL, KVL, ROPE = 384, 256, 64
WIN = QL + KVL + ROPE
NK = 6
EPS = 1e-6
ATT_SCALE = float((128 + ROPE) ** -0.5)


class Chain:

    def __init__(self, eng, sem):
        self.eng, self.sem, self.base, self.n = eng, sem, 0, 0

    def link(self, ins):
        self.n += 1
        ins.then_inc(self.sem, 1)
        self.eng.wait_ge(self.sem, self.base + self.n)

    def enter(self, i, first, per):
        self.saved, self.per, self.turns_n = self.n, per, 0
        self.base, self.n = (i - first) * per + self.saved, 0

    def leave(self, turns):
        assert self.n == self.per, (self.n, self.per)
        self.base, self.n = 0, self.saved + turns * self.per


def trunk(nc, a, o, STAGE=9):
    ctx = ExitStack()
    with ctx:
        def sb(name, shape):
            return ctx.enter_context(nc.sbuf_tensor(name, shape, F32))

        def sem(name):
            return ctx.enter_context(nc.semaphore(name))

        X = sb("X", [P, NT, D])
        B1 = sb("B1", [P, NT, D])
        B2 = sb("B2", [P, KD * TOK])
        W = sb("W", [P, 6, SLOT])
        GATE = sb("GATE", [P, 2, D])
        IDENT = sb("IDENT", [P, P])
        ONES = sb("ONES", [P, P])
        ADA = sb("ADA", [P, DEPTH, 6, KD, 2])
        NCOL = sb("NCOL", [P, 88])
        BCOL = sb("BCOL", [P, DEPTH, 48])
        CS = sb("CS", [P, 2, NLAT, ROPE])
        SLOTNO = sb("SLOTNO", [P, CAP])
        STEP1 = sb("STEP1", [P, LAT])
        SMALL = sb("SMALL", [P, 128])
        REGION = sb("REGION", [P, 8960])

        HT = B2[:].rearrange("p (k t) -> p k t", k=KD)
        YB2 = B2[:].rearrange("p (t d) -> p t d", t=NT)
        ps = ctx.enter_context(nc.psum_tensor("ps", [P, 8, HALF], F32))

        small_at = [0]

        def small(n):
            small_at[0] += n
            assert small_at[0] <= 128
            return SMALL[:, small_at[0] - n:small_at[0]]

        SS, MS, RSTD = small(NT), small(NT), small(NT)
        NHALF = small(NT)
        LG = small(8)
        NLGB, LGB513 = small(4), small(4)
        LU, LV, LW = small(8), small(8), small(8)
        TPOS = small(2)
        KDEC = small(2)
        BST, MV, RV, RSY = small(6), small(2 * NT), small(NT), small(NT)
        EPSC, IDLE = small(1), small(1)

        def carve(tensor, width):
            at = [0]

            def take(*shape):
                n = 1
                for s in shape:
                    n *= s
                at[0] += n
                assert at[0] <= width, (at[0], width)
                view = tensor[:, at[0] - n:at[0]]
                if len(shape) == 2:
                    return view.rearrange("p (a b) -> p a b", a=shape[0])
                if len(shape) == 3:
                    return view.rearrange("p (a b c) -> p a b c", a=shape[0], b=shape[1])
                if len(shape) == 4:
                    return view.rearrange("p (a b c e) -> p a b c e", a=shape[0], b=shape[1], c=shape[2])
                return view
            return take

        take = carve(REGION, 8960)
        RAW = take(3, P)
        AROW = take(2, HALF)
        take = carve(REGION, 8960)
        STATE = take(2, HALF)
        QT, KT = take(2, TOK), take(2, TOK)
        SILG = take(2, HALF)
        CROSS = take(2, LAT)
        YT = take(2, 4, P)
        DEC = take(896)
        WLAST = W[:].rearrange("p s n -> p (s n)")[:, 4 * SLOT:6 * SLOT]
        take = carve(WLAST, 2 * SLOT)
        V = take(NT, DV)
        SC = take(NLAT, LAT)
        SCP = take(P)
        S0 = take(2, 2, DV)
        KP = take(2, DK)
        DIFF = take(896)
        take = carve(GATE[:].rearrange("p c d -> p (c d)"), 2 * D)
        QX = take(2, 2, 2, P)
        YN = take(2, HALF)
        DTMP = QX.rearrange("p a b c e -> p (a b c e)")[:, 0:896]
        take = carve(REGION, 8960)
        XE = take(D)
        XEP = take(D)
        XET = take(2, KD, ROWS)
        HID = take(D)
        HTE = take(KD, ROWS)
        YE = take(D)
        YEP = take(D)
        OH = take(NT, 2, CAP)
        OHG = take(NT, 2, CAP)
        mix_more = carve(GATE[:].rearrange("p c d -> p (c d)"), 2 * D)
        CT = mix_more(NT, P)
        WR = mix_more(KD, NE)
        AFF = mix_more(NT, NE)
        POST = mix_more(NT, NE)
        LGS = mix_more(NT, NE)
        MX = mix_more(NT)
        RC = mix_more(NT)
        M8 = mix_more(8)
        WK, SEL, POS = XE[:, 0:TOK], XEP[:, 0:TOK], HID[:, 0:TOK]

        take = carve(REGION, 8960)
        KVT = take(2, NK * P)
        KRT = take(NK * P)
        KNT = take(2, NK * P)
        QNT = take(2, TOK)
        VP = take(D)
        PR = take(2, LAT + P)
        PTP = take(P)
        KVG = take(KVL)
        CKC = take(KVL)
        LSS, LMS, LRS = take(2 * NT), take(2 * NT), take(2 * NT)
        RMX, RNM, RSM, RRC = take(2), take(2), take(2), take(2)
        KRD = KNT.rearrange("p b n -> p (b n)")[:, 0:NK * P].rearrange("p (t n) -> p t n", t=NK)
        RA, RB = (QNT.rearrange("p b n -> p (b n)")[:, x * HALF:(x + 1) * HALF] for x in range(2))
        CKO = PR[:, 0, 0:KVL]
        take = carve(WLAST, 2 * SLOT)
        LATN = take(NT, WIN)
        QLT = take(3, TOK)
        QRT = take(4, TOK)
        QR = WLAST[:, 0:NT * HALF].rearrange("p (t n) -> p t n", t=NT)
        PT = WLAST[:, 0:NT * LAT].rearrange("p (t n) -> p t n", t=NT)
        OT = B2[:].rearrange("p (h t) -> p h t", h=MH)
        WIN2 = [W[:, s, 0:4 * WIN].rearrange("p (k n) -> p k n", k=4) for s in (0, 1)]
        WQB = [W[:, s, 0:3 * 768].rearrange("p (k h n) -> p k h n", k=3, h=4) for s in (2, 3)]
        WKV = W[:, 0, :].rearrange("p (k h n) -> p k h n", k=2, h=MH)

        rows_in, x_in, dec_in, cs_in = sem("rows_in"), sem("x_in"), sem("dec_in"), sem("cs_in")
        w_in = [sem(f"w_in{s}") for s in range(6)]
        const_ready = sem("const_ready")
        cols_tr, cols_ev = sem("cols_tr"), sem("cols_ev")
        cond_ready = sem("cond_ready")
        ada_mm, ada_ev, ada_tr, ada_col = sem("ada_mm"), sem("ada_ev"), sem("ada_tr"), sem("ada_col")
        ada_ready = sem("ada_ready")
        dve_chain, pool_chain = sem("dve_chain"), sem("pool_chain")
        nt_ss, nt_rstd, nt_xn, nt_tr = sem("nt_ss"), sem("nt_rstd"), sem("nt_xn"), sem("nt_tr")
        nt_evd, nt_eva = sem("nt_evd"), sem("nt_eva")
        gate_diag, gate_mm, gate_ev = sem("gate_diag"), sem("gate_mm"), sem("gate_ev")
        ru_ss, ru_rstd, x_ready = sem("ru_ss"), sem("ru_rstd"), sem("x_ready")
        stored = sem("stored")
        s0_in = sem("s0_in")
        lu_ready, lg_ready, te_ready, dec_ready = sem("lu_ready"), sem("lg_ready"), sem("te_ready"), sem("dec_ready")
        qk_mm, qk_ev, v_mm, v_ev = sem("qk_mm"), sem("qk_ev"), sem("v_mm"), sem("v_ev")
        sc_mm, sc_ev, kp_mm, kp_ev = sem("sc_mm"), sem("sc_ev"), sem("kp_mm"), sem("kp_ev")
        qx_ready, y_mm, g_mm, silg = sem("qx_ready"), sem("y_mm"), sem("g_mm"), sem("silg")
        var_ready, rsy_ready, yn_done = sem("var_ready"), sem("rsy_ready"), sem("yn_done")
        yt_mm, yt_ev, out_mm, out_acc = sem("yt_mm"), sem("yt_ev"), sem("out_mm"), sem("out_acc")
        st_mm, st_ev = sem("st_mm"), sem("st_ev")
        st_out = [sem("st_out0"), sem("st_out1")]

        MLAN = ("ctx_in", "lat_mm", "lat_ev", "lat_ss", "lat_rstd", "lat_n", "kr_ready", "cko", "new_out",
                "ql_tr", "ql_ev", "kv_tr", "kv_ev", "qr_mm", "qr_ev", "qr_rot", "qrt_tr", "qrt_ev", "vv_mm", "vv_ev",
                "kn_mm", "kn_ev", "s_mm", "nm", "e_done", "pr", "pt_tr", "pt_ev", "o_mm", "o_ev", "mo_mm", "mo_ev")
        MA = {n: sem("att_" + n) for n in MLAN}

        def act_copy(out, in_, scale=1.0):
            return nc.scalar.activation(out, in_, ACT.Copy, scale=scale)

        NPRE, NPOST, COND, QN, KVN = 0, 32, 64, 80, 83
        COLS = 85

        def norm_col(kind, layer, sub):
            at = (NPRE if kind == "pre" else NPOST) + (layer * 2 + sub) * KD
            return NCOL[:, at:at + KD]

        def scale_col(layer, sub, k, c):
            return ADA[:, layer, 3 * sub + 1, k, c:c + 1]

        def shift_col(layer, sub, k, c):
            return ADA[:, layer, 3 * sub, k, c:c + 1]

        MIXN = ("lg_mm", "lgs", "ex", "aff", "afft", "pos_tr", "post", "oh", "ohg",
                "ga_mm", "gb_mm", "da_mm", "db_mm", "sil", "h", "t_mm", "t_ev", "y_ev",
                "ct_mm", "ct_ev", "c_mm", "c_ev", "x_mm", "x_ev", "xt_mm", "xt_ev", "zero")
        MS_ = {n: sem("mix_" + n) for n in MIXN}
        wr_in = sem("wr_in")
        per_layer = dict(lg_mm=1, lgs=1, ex=1, aff=1, afft=1, pos_tr=1, post=1, oh=PAIRS, ohg=PAIRS,
                         ga_mm=NE, gb_mm=NE, da_mm=NE, db_mm=NE, sil=NE, h=NE, t_mm=2 * NE,
                         t_ev=2 * NE, y_ev=NE, ct_mm=2 * PAIRS, ct_ev=2 * PAIRS, c_mm=10 * PAIRS,
                         c_ev=10 * PAIRS, x_mm=4 * PAIRS, x_ev=4 * PAIRS, xt_mm=4 * PAIRS,
                         xt_ev=4 * PAIRS, zero=1)

        ada_w = a["ada_w"].rearrange("l (k p) n -> l p k n", p=P)
        ret_in = a["ret_w_in"][0].rearrange("(k p) n -> p k n", p=P)
        ret_out = a["ret_w_out"][0].rearrange("(h c p) n -> h p c n", p=P, c=4)
        W8 = W[:].rearrange("p s (k n) -> p s k n", k=KD)
        W4 = W[:].rearrange("p s (k n) -> p s k n", k=4)
        WQK = W[:, 0, :].rearrange("p (w k n) -> p w k n", w=2, k=KD)

        ADA_LOADS = 2 * ADA_CHUNKS // 6
        RET0 = ADA_LOADS
        MLA_LOADS = [2, 2, 2, 1, 0, 0]
        BEFORE_MIX = [[RET0 + 2 * HEADS, RET0 + HEADS, RET0 + HEADS, RET0 + HEADS, RET0, RET0]]
        BEFORE_MLA = [n + NE for n in BEFORE_MIX[0]]
        BEFORE_MIX.append([n + m for n, m in zip(BEFORE_MLA, MLA_LOADS)])

        block = ctx.enter_context(nc.Block())

        @block.sync
        def _(sp):
            for e, w in enumerate(("ret_decay_fwd", "ret_decay_bwd")):
                sp.dma_start(LU[:, 4 * e:4 * e + 4], a[w].to_broadcast([P, 4])).then_inc(dec_in, 16)
            sp.dma_start(RAW[0:32, 0, :], a["norm_pre"].rearrange("l s (k p) -> (l s k) p", p=P)).then_inc(rows_in, 16)
            sp.dma_start(RAW[32:64, 0, :], a["norm_post"].rearrange("l s (k p) -> (l s k) p", p=P)).then_inc(rows_in, 16)
            sp.dma_start(RAW[64:72, 0, :], a["c"].rearrange("b (k p) -> (b k) p", p=P)).then_inc(rows_in, 16)
            sp.dma_start(RAW[72:80, 0, :], a["c_ctx"].rearrange("(k p) -> k p", p=P)).then_inc(rows_in, 16)
            sp.dma_start(RAW[80:83, 0, :], a["mla_q_norm"].rearrange("l (k p) -> (l k) p", p=P)).then_inc(rows_in, 16)
            sp.dma_start(RAW[83:85, 0, :], a["mla_kv_norm"].rearrange("l (k p) -> (l k) p", p=P)).then_inc(rows_in, 16)
            for layer in range(DEPTH):
                sp.dma_start(RAW[0:48, 1 + layer, :], a["ada_b"][layer].rearrange("(k p) -> k p", p=P)).then_inc(rows_in, 16)
            for layer in range(DEPTH):
                for j in range(2):
                    for s in range(6):
                        n = layer * 2 + j
                        if n:
                            sp.wait_ge(ada_mm, 6 * (n - 1) + s + 1)
                        lo = (6 * j + s) * HALF
                        sp.dma_start(W8[:, s], ada_w[layer, :, :, lo:lo + HALF]).then_inc(w_in[s], 16)
                        if n == 0 and s == 1:
                            sp.dma_start(X[:, 0:NLAT, :], a["x_sample"][0].rearrange("(t p) d -> p t d", p=P)).then_inc(x_in, 16)
                            sp.dma_start(X[:, NLAT, :], a["x_prompt"][0]).then_inc(x_in, 16)
                            sp.dma_start(CS[:], a["rotary"].rearrange("c (t p) r -> p c t r", p=P)).then_inc(cs_in, 16)

            def ret_loads(h, first):
                sp.wait_ge(ada_mm, 19) if first else sp.wait_ge(qk_mm, 4 * h)
                for w in range(2):
                    sp.dma_start(WQK[:, w], ret_in[:, :, bass.ds(w * D + h * DK, DK)]).then_inc(w_in[0], 16)
                sp.wait_ge(ada_mm, 20) if first else sp.wait_ge(v_mm, NT * h)
                sp.dma_start(W8[:, 1], ret_in[:, :, bass.ds(2 * D + h * DV, DV)]).then_inc(w_in[1], 16)
                sp.wait_ge(ada_mm, 24) if first else sp.wait_ge(y_mm, NT * h)
                for e, st in enumerate(("state_ret_fwd", "state_ret_bwd")):
                    sp.dma_start(S0[:, e], a[st].rearrange("a b h (m p) e -> (a b h) p m e", p=P)[bass.ds(h, 1)][0]).then_inc(s0_in, 16)
                sp.wait_ge(ada_mm, 21) if first else sp.wait_ge(g_mm, NT * h)
                sp.dma_start(W8[:, 2], ret_in[:, :, bass.ds(2 * D + HEADS * DV + h * DV, DV)]).then_inc(w_in[2], 16)
                sp.wait_ge(ada_mm, 22) if first else sp.wait_ge(out_mm, 2 * NT * h)
                sp.dma_start(W4[:, 3], ret_out[bass.ds(h, 1)][0]).then_inc(w_in[3], 16)

            ret_loads(0, True)
            with sp.Fori(1, HEADS) as h:
                ret_loads(h, False)

            def mix_loads(layer, e, first):
                gate, up, down = (a[n][layer].rearrange("e (g k p) n -> e g p k n", p=P, k=4)
                                  for n in ("moe_w_gate", "moe_w_up", "moe_w_down"))
                b = {n: layer * v for n, v in per_layer.items()}
                for half, done in ((0, "ga_mm"), (1, "gb_mm")):
                    for w, src in ((0, gate), (2, up)):
                        slot = w + half
                        if first and layer == 0:
                            sp.wait_ge(*((qk_mm, 4 * HEADS), (v_mm, NT * HEADS), (g_mm, NT * HEADS), (out_mm, 2 * NT * HEADS))[slot])
                        if first and layer == 1:
                            mla_last(sp, slot)
                        if not first:
                            sp.wait_ge(MS_[done], b[done] + e)
                        sp.dma_start(W4[:, slot], src[bass.ds(e, 1)][0, half]).then_inc(w_in[slot], 16)
                for half, done in ((0, "da_mm"), (1, "db_mm")):
                    slot = 4 + half
                    if first and layer == 0:
                        sp.wait_ge(out_acc, 2 * NT * HEADS)
                        sp.wait_ge(st_mm, 4 * HEADS)
                    if first and layer == 1:
                        mla_last(sp, slot)
                    if not first:
                        sp.wait_ge(MS_[done], b[done] + e)
                    sp.dma_start(W4[:, slot], down[bass.ds(e, 1)][0, half]).then_inc(w_in[slot], 16)

            def mix_all(layer):
                sp.wait_ge(x_ready, (2 * layer + 1) * NT)
                sp.dma_start(WR, a["moe_w_router"][layer].rearrange("(k p) e -> p k e", p=P)).then_inc(wr_in, 16)
                mix_loads(layer, 0, True)
                with sp.Fori(1, NE) as e:
                    mix_loads(layer, e, False)

            def mla_last(sp, slot):
                sp.wait_ge(*((MA["kn_mm"], 2 * MH), (MA["mo_mm"], 2 * NT), (MA["mo_mm"], 2 * NT), (MA["kn_mm"], 2 * MH),
                             (MA["mo_mm"], 1), (MA["mo_mm"], 1))[slot])

            def mla_loads():
                sp.wait_ge(x_ready, 2 * NT)
                sp.dma_start(CKC, a["cache_mla_ckv"][0, 0]).then_inc(MA["ctx_in"], 16)
                for j in range(2):
                    sp.dma_start(KRD[:, 0, j * ROPE:(j + 1) * ROPE], a["cache_mla_krope"][0, 0]).then_inc(MA["ctx_in"], 16)
                sp.dma_start(KVG, a["mla_kv_norm"].to_broadcast([P, KVL])).then_inc(MA["ctx_in"], 16)
                wi = a["mla_w_in"][0].rearrange("(g k p) n -> g p k n", p=P, k=4)
                wq = a["mla_w_q_b"][0].rearrange("(k p) (g n) -> g p k n", p=P, g=2)
                wo = a["mla_w_out"][0].rearrange("(g k p) n -> g p k n", p=P, k=4)
                sp.wait_ge(MS_["gb_mm"], NE)
                for g in range(2):
                    sp.dma_start(WIN2[g], wi[g]).then_inc(w_in[g], 16)
                for g in range(2):
                    sp.dma_start(W[:, 2 + g, 0:2304].rearrange("p (k n) -> p k n", k=3), wq[g]).then_inc(w_in[2 + g], 16)
                sp.wait_ge(MA["lat_mm"], NT)
                sp.dma_start(W[:, 0, :].rearrange("p (k n) -> p k n", k=2),
                             a["mla_w_kv_b"][0].rearrange("(k p) n -> p k n", p=P)).then_inc(w_in[0], 16)
                sp.dma_start(W4[:, 1], wo[0]).then_inc(w_in[1], 16)
                sp.wait_ge(MA["lat_ev"], NT)
                sp.dma_start(o["new_krope"][0, 0], LATN[:, NLAT, QL + KVL:WIN]).then_inc(MA["new_out"], 16)
                sp.wait_ge(MA["cko"], 1)
                sp.dma_start(o["new_ckv"][0, 0], CKO).then_inc(MA["new_out"], 16)
                sp.wait_ge(MA["kn_mm"], MH)
                sp.dma_start(W4[:, 2], wo[1]).then_inc(w_in[2], 16)

            if STAGE >= 2:
                mix_all(0)
            if STAGE >= 3:
                mla_loads()
                mix_all(1)
            n_x = {1: 1, 2: 2, 3: 4}[STAGE]
            sp.wait_ge(x_ready, NT * n_x)
            sp.dma_start(o["y_sample"][0].rearrange("(t p) d -> p t d", p=P), X[:, 0:NLAT, :]).then_inc(stored, 16)
            sp.dma_start(o["y_prompt"][0], X[:, NLAT, :]).then_inc(stored, 16)
            sp.wait_ge(stored, 32)

        @block.gpsimd
        def _(pool):
            chain = Chain(pool, pool_chain)
            chain.link(nc.gpsimd.memset(IDENT[:], 0.0))
            nc.gpsimd.affine_select(out=IDENT[:], in_=IDENT[:], compare_op=ALU.not_equal, fill=1.0,
                                    base=0, pattern=[[-1, P]], channel_multiplier=1).then_inc(const_ready, 1)
            nc.gpsimd.memset(ONES[:], 1.0).then_inc(const_ready, 1)
            nc.gpsimd.memset(EPSC, EPS).then_inc(const_ready, 1)
            nc.gpsimd.memset(NHALF, -0.5).then_inc(const_ready, 1)
            kw = dict(allow_small_or_imprecise_dtypes=True)
            nc.gpsimd.iota(SLOTNO[:], [[1, CAP]], base=1, channel_multiplier=0, **kw).then_inc(const_ready, 1)
            nc.gpsimd.iota(STEP1[:], [[1, LAT]], base=1, channel_multiplier=0, **kw).then_inc(const_ready, 1)
            nc.gpsimd.iota(TPOS[:, 0:1], [[1, 1]], base=P - 1, channel_multiplier=-1, **kw).then_inc(const_ready, 1)
            nc.gpsimd.iota(TPOS[:, 1:2], [[1, 1]], base=0, channel_multiplier=1, **kw).then_inc(const_ready, 1)
            pool.wait_ge(ada_mm, 24)
            nc.gpsimd.iota(DIFF, [[1, 896]], base=-384, channel_multiplier=-1, **kw).then_inc(const_ready, 1)

            def rstd(source, needs, out, ready, n):
                pool.wait_ge(source, needs)
                chain.link(nc.gpsimd.tensor_scalar(MS, SS, 1.0 / D, EPS, ALU.mult, ALU.add))
                nc.gpsimd.tensor_tensor(out, MS, NHALF, ALU.pow).then_inc(ready, 1)

            rstd(nt_ss, NT, RSTD, nt_rstd, 0)

            def ret_head(h):
                for t in range(NT):
                    pool.wait_ge(var_ready, NT * h + t + 1)
                    chain.link(nc.gpsimd.tensor_tensor(RV[:, t:t + 1], MV[:, 2 * t + 1:2 * t + 2], EPSC, ALU.add))
                    nc.gpsimd.tensor_tensor(RSY[:, t:t + 1], RV[:, t:t + 1], NHALF[:, 0:1], ALU.pow).then_inc(rsy_ready, 1)
            ret_head(0)
            with pool.Fori(1, HEADS) as h:
                chain.enter(h, 1, NT)
                ret_head(h)
            chain.leave(HEADS - 1)
            rstd(ru_ss, NT, RSTD, ru_rstd, 0)

            def mix_pool(layer):
                rstd(nt_ss, NT * (2 * layer + 2), RSTD, nt_rstd, 0)
                pool.wait_ge(MS_["lg_mm"], layer + 1)
                nc.gpsimd.memset(YB2, 0.0).then_inc(MS_["zero"], 1)
                rstd(ru_ss, NT * (2 * layer + 2), RSTD, ru_rstd, 0)

            if STAGE >= 2:
                mix_pool(0)
            if STAGE >= 3:
                rstd(nt_ss, 3 * NT, RSTD, nt_rstd, 0)
                pool.wait_ge(MA["lat_ss"], 2 * NT)
                nc.gpsimd.tensor_scalar(LMS[:, 0:NT], LSS[:, 0:NT], 1.0 / QL, EPS, ALU.mult, ALU.add)
                chain.link(nc.gpsimd.tensor_scalar(LMS[:, NT:2 * NT], LSS[:, NT:2 * NT], 1.0 / KVL, EPS, ALU.mult, ALU.add))
                for j in range(2):
                    nc.gpsimd.tensor_tensor(LRS[:, j * NT:(j + 1) * NT], LMS[:, j * NT:(j + 1) * NT], NHALF, ALU.pow).then_inc(MA["lat_rstd"], 1)
                rstd(ru_ss, 3 * NT, RSTD, ru_rstd, 0)
                mix_pool(1)
        @block.scalar
        def _(act):
            act.wait_ge(lu_ready, 1)
            nc.scalar.activation(LV, LV, ACT.Exp).then_inc(lu_ready, 1)
            act.wait_ge(cols_tr, 3)
            act_copy(BCOL[:, 0, :], ps[:, 1, 0:48]).then_inc(cols_ev, 1)
            act_copy(BCOL[:, 1, :], ps[:, 2, 0:48]).then_inc(cols_ev, 1)
            act_copy(NCOL[:, 0:COND], ps[:, 0, 0:COND]).then_inc(cols_ev, 1)
            act_copy(NCOL[:, QN:COLS], ps[:, 0, QN:COLS]).then_inc(cols_ev, 1)
            nc.scalar.activation(NCOL[:, COND:QN], ps[:, 0, COND:QN], ACT.Silu).then_inc(cond_ready, 1)
            for n in range(2 * ADA_CHUNKS):
                act.wait_ge(ada_mm, n + 1)
                if n >= 2:
                    act.wait_ge(ada_tr, n - 1)
                act_copy(AROW[0:2, n % 2, :], ps[0:2, n % 2, :]).then_inc(ada_ev, 1)

            def norm_act(n, layer, sub, x_sem, x_needs):
                for t in range(NT):
                    act.wait_ge(x_sem, x_needs(t))
                    nc.scalar.activation(B1[:, t, :], X[:, t, :], ACT.Square, accum_out=SS[:, t:t + 1]).then_inc(nt_ss, 1)
                for t in range(NT):
                    act.wait_ge(nt_tr, 10 * n + 2 * t + 2)
                    c = t // NLAT
                    for k in range(4, 8):
                        last = nc.scalar.activation(HT[:, k, t * P:(t + 1) * P], ps[:, 5 + 2 * (t % 2), (k - 4) * P:(k - 3) * P],
                                                    ACT.Identity, scale=scale_col(layer, sub, k, c), bias=shift_col(layer, sub, k, c))
                    last.then_inc(nt_eva, 1)

            def gates_act(n):
                for j in range(4):
                    act.wait_ge(gate_mm, 4 * n + j + 1)
                    act_copy(GATE[:, j // 2, (j % 2) * HALF:(j % 2 + 1) * HALF], ps[:, j, :]).then_inc(gate_ev, 1)

            def update_act(n, Y, other, ready, needs):
                act.wait_ge(ready, needs)
                for t in range(NT):
                    nc.scalar.activation(other[:, t, :], Y[:, t, :], ACT.Square, accum_out=SS[:, t:t + 1]).then_inc(ru_ss, 1)

            act.wait_ge(ada_ready, 1)
            norm_act(0, 0, 0, x_in, lambda t: 32)

            def ret_head(h, first):
                act.wait_ge(te_ready, h + 1)
                nc.scalar.activation(DEC, DEC, ACT.Exp).then_inc(dec_ready, 1)
                nc.scalar.activation(CROSS[:, 0, :], STEP1[:], ACT.Exp, scale=LG[:, bass.ds(h, 1)]).then_inc(dec_ready, 1)
                nc.scalar.activation(CROSS[:, 1, :], STEP1[:], ACT.Exp, scale=NLGB[:, bass.ds(h, 1)], bias=LGB513[:, bass.ds(h, 1)]).then_inc(dec_ready, 1)
                nc.scalar.activation(KDEC[:, 0:1], TPOS[:, 0:1], ACT.Exp, scale=LG[:, bass.ds(h, 1)]).then_inc(dec_ready, 1)
                nc.scalar.activation(KDEC[:, 1:2], TPOS[:, 1:2], ACT.Exp, scale=LG[:, bass.ds(h + 4, 1)]).then_inc(dec_ready, 1)
                for u in range(4):
                    act.wait_ge(qk_mm, 4 * h + u + 1)
                    dst, scale = (QT, 1.0) if u < 2 else (KT, DK ** -0.5)
                    b = 2 * (u % 2)
                    act_copy(dst[:, u % 2, 0:LAT], ps[:, b, :], scale)
                    act_copy(dst[:, u % 2, LAT:TOK], ps[:, b + 1, 0:P], scale).then_inc(qk_ev, 1)
                for t in range(NT):
                    act.wait_ge(v_mm, NT * h + t + 1)
                    act_copy(V[:, t, :], ps[:, 4 + t % 2, :]).then_inc(v_ev, 1)
                for t in range(NT + 1):
                    if t < NT:
                        act.wait_ge(g_mm, NT * h + t + 1)
                        if t >= 2 or not first:
                            act.wait_ge(yn_done, NT * h + t - 1 if t >= 2 else NT * h)
                        nc.scalar.activation(SILG[:, t % 2, :], ps[:, 2 + t % 2, :], ACT.Silu).then_inc(silg, 1)
                    if t >= 1:
                        u = t - 1
                        act.wait_ge(yt_mm, NT * h + u + 1)
                        if u >= 2 or not first:
                            act.wait_ge(out_mm, 2 * NT * h + 2 * (u - 1) if u >= 2 else 2 * NT * h)
                        act_copy(YT[:, u % 2], ps[:, 4 + u % 2, :].rearrange("p (c t) -> p c t", c=4)).then_inc(yt_ev, 1)
                for j in range(4):
                    act.wait_ge(st_mm, 4 * h + j + 1)
                    if j >= 2 or not first:
                        act.wait_ge(st_out[j % 2], 16 * (2 * h + j // 2))
                    act_copy(STATE[:, j % 2, :], ps[:, j, :]).then_inc(st_ev, 1)
                    act.wait_ge(st_ev, 4 * h + j + 1)
                    dst = o[("state_fwd", "state_bwd")[j // 2]].rearrange("a b h (m p) e -> (a b h) m p e", p=P)
                    act.dma_start(dst[bass.ds(h, 1)][0, j % 2], STATE[:, j % 2]).then_inc(st_out[j % 2], 16)

            ret_head(0, True)
            with act.Fori(1, HEADS) as h:
                ret_head(h, False)
            act.wait_ge(st_out[0], 16 * 2 * HEADS)
            act.wait_ge(st_out[1], 16 * 2 * HEADS)
            gates_act(0)
            update_act(0, B1, YB2, out_acc, 2 * NT * HEADS)

            def mix_act(layer):
                b = {n: layer * v for n, v in per_layer.items()}
                norm_act(2 * layer + 1, layer, 1, x_ready, lambda t: NT * 2 * layer + t + 1)
                act.wait_ge(MS_["lgs"], b["lgs"] + 1)
                nc.scalar.activation(LGS, LGS, ACT.Exp).then_inc(MS_["ex"], 1)

                def gathered(pair, u):
                    for half in range(2):
                        act.wait_ge(MS_["x_mm"], b["x_mm"] + 4 * pair + 2 * u + half + 1)
                        act_copy((XE, XEP)[u][:, half * HALF:(half + 1) * HALF], ps[:, 6 + half, :]).then_inc(MS_["x_ev"], 1)

                def sil(e):
                    act.wait_ge(MS_["gb_mm"], b["gb_mm"] + e + 1)
                    nc.scalar.activation(HID[0:ROWS, :].rearrange("p (a n) -> p a n", a=2), ps[0:ROWS, 0:2, :], ACT.Silu).then_inc(MS_["sil"], 1)

                def hidden(e):
                    for half in range(2):
                        act.wait_ge(MS_["t_mm"], b["t_mm"] + 2 * e + half + 1)
                        act_copy(HTE[:, 4 * half:4 * half + 4, :], ps[:, 6 + half, 0:4 * ROWS].rearrange("p (c r) -> p c r", c=4)).then_inc(MS_["t_ev"], 1)

                def expert_out(e, odd):
                    act.wait_ge(MS_["db_mm"], b["db_mm"] + e + 1)
                    at = 64 * odd
                    act_copy(YE[at:at + CAP, :].rearrange("p (a n) -> p a n", a=2), ps[0:CAP, 4:6, :])
                    act_copy(YEP[at:at + CAPP, :].rearrange("p (a n) -> p a n", a=2), ps[CAP:ROWS, 4:6, :]).then_inc(MS_["y_ev"], 1)

                def combine_rows(pair):
                    for half in range(2):
                        act.wait_ge(MS_["ct_mm"], b["ct_mm"] + 2 * pair + half + 1)
                        if half == 0:
                            act_copy(CT[:, 0:4, :], ps[:, 6, :].rearrange("p (t n) -> p t n", t=4)).then_inc(MS_["ct_ev"], 1)
                        else:
                            act_copy(CT[:, 4, :], ps[:, 7, 0:P]).then_inc(MS_["ct_ev"], 1)

                act.wait_ge(MS_["post"], b["post"] + 1)
                gathered(0, 0)
                gathered(0, 1)

                def turn(p, first, last):
                    sil(2 * p)
                    if not first:
                        expert_out(2 * p - 1, 1)
                    hidden(2 * p)
                    if not first:
                        combine_rows(p - 1)
                    if not last:
                        gathered(p + 1, 0)
                    sil(2 * p + 1)
                    if not last:
                        gathered(p + 1, 1)
                    expert_out(2 * p, 0)
                    hidden(2 * p + 1)

                turn(0, True, False)
                with act.Fori(1, PAIRS - 1) as p:
                    turn(p, False, False)
                turn(PAIRS - 1, False, True)
                expert_out(NE - 1, 1)
                combine_rows(PAIRS - 1)
                n = 2 * layer + 1
                act.wait_ge(MS_["c_mm"], b["c_mm"] + 10 * PAIRS)
                gates_act(n)
                update_act(n, YB2, B1, MS_["c_ev"], b["c_ev"] + 10 * PAIRS)

            def mla_act():
                norm_act(2, 1, 0, x_ready, lambda t: NT + t + 1)
                for t in range(NT):
                    act.wait_ge(MA["lat_mm"], t + 1)
                    b = 2 * (t % 2)
                    act_copy(LATN[:, t, :], ps[:, b:b + 2, :].rearrange("p a n -> p (a n)")[:, 0:WIN]).then_inc(MA["lat_ev"], 1)
                    act.wait_ge(MA["lat_ev"], t + 1)
                    nc.scalar.activation(B1[:, t, 0:QL], LATN[:, t, 0:QL], ACT.Square, accum_out=LSS[:, t:t + 1]).then_inc(MA["lat_ss"], 1)
                    nc.scalar.activation(B1[:, t, QL:QL + KVL], LATN[:, t, QL:QL + KVL], ACT.Square, accum_out=LSS[:, NT + t:NT + t + 1]).then_inc(MA["lat_ss"], 1)
                for kt in range(NK):
                    act.wait_ge(MA["kv_tr"], kt + 1)
                    for c in range(2):
                        dst, src = KVT[:, c, kt * P:(kt + 1) * P], ps[:, 6 + kt % 2, c * P:(c + 1) * P]
                        if kt == 0:
                            act_copy(dst, src)
                        else:
                            nc.scalar.activation(dst, src, ACT.Identity, scale=NCOL[:, KVN + c:KVN + c + 1])
                    act_copy(KRT[:, kt * P:(kt + 1) * P], ps[:, 6 + kt % 2, 2 * P:3 * P]).then_inc(MA["kv_ev"], 1)
                act.wait_ge(MA["new_out"], 32)
                for t in range(NT):
                    act.wait_ge(MA["qr_mm"], t + 1)
                    act_copy(QR[:, t, :], ps[:, t % 4, :]).then_inc(MA["qr_ev"], 1)
                for kt in range(NK):
                    for half in range(2):
                        act.wait_ge(MA["vv_mm"], 2 * kt + half + 1)
                        dst = B1[:, kt, half * HALF:(half + 1) * HALF] if kt < NT else VP[:, half * HALF:(half + 1) * HALF]
                        act_copy(dst, ps[:, 6 + half, :]).then_inc(MA["vv_ev"], 1)
                for t in range(NT):
                    act.wait_ge(MA["qrt_tr"], t + 1)
                    act_copy(QRT[:, :, t * P:(t + 1) * P], ps[:, 4 + t % 2, :].rearrange("p (c t) -> p c t", c=4)).then_inc(MA["qrt_ev"], 1)

                def exps(h, t):
                    n = NT * h + t
                    act.wait_ge(MA["nm"], n + 1)
                    if n >= 2:
                        act.wait_ge(MA["pt_tr"], n - 1)
                    b = (4, 6, 4, 6, 4)[t]
                    width = LAT + P if t < NLAT else P
                    src = ps[:, b:b + 2, :].rearrange("p a n -> p (a n)")[:, 0:width]
                    nc.scalar.activation(PR[:, n % 2, 0:width], src, ACT.Exp, scale=ATT_SCALE, bias=RNM[:, n % 2:n % 2 + 1],
                                         accum_out=RSM[:, n % 2:n % 2 + 1]).then_inc(MA["e_done"], 1)

                for h in range(MH):
                    act.wait_ge(MA["kn_mm"], 2 * h + 1)
                    act_copy(KNT[:, h % 2, :], ps[:, 0:2, :].rearrange("p a n -> p (a n)")[:, 0:NK * P]).then_inc(MA["kn_ev"], 1)
                    act.wait_ge(MA["kn_mm"], 2 * h + 2)
                    act_copy(QNT[:, h % 2, :], ps[:, 2:4, :].rearrange("p a n -> p (a n)")[:, 0:TOK]).then_inc(MA["kn_ev"], 1)
                    exps(h, 0)
                    for t in range(NT):
                        if t + 1 < NT:
                            exps(h, t + 1)
                        act.wait_ge(MA["pt_tr"], NT * h + t + 1)
                        if t < NLAT:
                            b = 2 * (t % 2)
                            src = ps[:, b:b + 2, :].rearrange("p a n -> p (a n)")[:, 0:LAT + P].rearrange("p (k q) -> p k q", q=P)
                            act_copy(PT[:, :, t * P:(t + 1) * P], src).then_inc(MA["pt_ev"], 1)
                        else:
                            act_copy(PTP, ps[:, 0, 0:P]).then_inc(MA["pt_ev"], 1)
                for t in range(NT):
                    for half in range(2):
                        act.wait_ge(MA["mo_mm"], 2 * t + half + 1)
                        act_copy(B1[:, t, half * HALF:(half + 1) * HALF], ps[:, 4 + 2 * (t % 2) + half, :]).then_inc(MA["mo_ev"], 1)
                gates_act(2)
                act.wait_ge(MA["mo_ev"], 2 * NT)
                update_act(2, B1, YB2, MA["mo_ev"], 2 * NT)

            if STAGE >= 2:
                mix_act(0)
            if STAGE >= 3:
                mla_act()
                mix_act(1)

        @block.vector
        def _(dve):
            chain = Chain(dve, dve_chain)
            V_ = nc.vector
            dve.wait_ge(dec_in, 32)
            chain.link(V_.tensor_scalar(LV, LU, -1.0, None, ALU.mult))
            chain.link(V_.tensor_tensor(LV, LV, LU, ALU.min))
            chain.link(V_.tensor_scalar(LU, LU, 0.0, None, ALU.min))
            V_.memset(LW, 0.0).then_inc(lu_ready, 1)
            dve.wait_ge(lu_ready, 2)
            chain.link(V_.tensor_scalar(LW, LV, 2.0, None, ALU.add))
            chain.link(V_.reciprocal(LW, LW))
            chain.link(V_.tensor_tensor(LV, LV, LW, ALU.mult))
            chain.link(V_.tensor_tensor(LW, LV, LV, ALU.mult))
            chain.link(V_.tensor_scalar(LG, LW, 1.0 / 17, 1.0 / 15, ALU.mult, ALU.add))
            for n in (13, 11, 9, 7, 5, 3, 1):
                chain.link(V_.tensor_tensor(LG, LG, LW, ALU.mult))
                chain.link(V_.tensor_scalar(LG, LG, 1.0 / n, None, ALU.add))
            chain.link(V_.tensor_tensor(LG, LG, LV, ALU.mult))
            chain.link(V_.scalar_tensor_tensor(LG, LG, -2.0, LU, ALU.mult, ALU.add))
            chain.link(V_.tensor_scalar(NLGB, LG[:, 4:8], -1.0, None, ALU.mult))
            chain.link(V_.tensor_scalar(LGB513, LG[:, 4:8], float(LAT + 1), None, ALU.mult))
            dve.wait_ge(cols_ev, 4)
            for n in range(2 * ADA_CHUNKS):
                dve.wait_ge(ada_tr, n + 1)
                layer, m = n // ADA_CHUNKS, n % ADA_CHUNKS
                cols = ADA[:, layer].rearrange("p j k c -> p (j k) c")[:, 4 * m:4 * m + 4, :]
                bias = BCOL[:, layer, 4 * m:4 * m + 4].unsqueeze(2).to_broadcast([P, 4, 2])
                V_.tensor_tensor(cols, ps[:, 2 + n % 2, 0:8].rearrange("p (k c) -> p k c", k=4), bias, ALU.add).then_inc(ada_col, 1)
            dve.wait_ge(ada_col, 2 * ADA_CHUNKS)
            for layer in range(DEPTH):
                for sub in range(2):
                    sc = ADA[:, layer, 3 * sub + 1]
                    V_.scalar_tensor_tensor(sc, sc, 1.0, norm_col("pre", layer, sub).unsqueeze(2).to_broadcast([P, KD, 2]), ALU.add, ALU.mult)
                    g = ADA[:, layer, 3 * sub + 2]
                    last = V_.tensor_tensor(g, g, norm_col("post", layer, sub).unsqueeze(2).to_broadcast([P, KD, 2]), ALU.mult)
            last.then_inc(ada_ready, 1)
            dve.wait_ge(ada_ready, 1)

            def norm_dve(n, layer, sub):
                dve.wait_ge(nt_rstd, n + 1)
                for t in range(NT):
                    V_.tensor_scalar(B1[:, t, :], X[:, t, :], RSTD[:, t:t + 1], None, ALU.mult).then_inc(nt_xn, 1)
                for t in range(NT):
                    dve.wait_ge(nt_tr, 10 * n + 2 * t + 1)
                    c = t // NLAT
                    for k in range(4):
                        last = V_.tensor_scalar(HT[:, k, t * P:(t + 1) * P], ps[:, 4 + 2 * (t % 2), k * P:(k + 1) * P],
                                                scale_col(layer, sub, k, c), shift_col(layer, sub, k, c), ALU.mult, ALU.add)
                    last.then_inc(nt_evd, 1)

            def gates_dve(n, layer, sub, diag):
                for j in range(4):
                    if j >= 1:
                        dve.wait_ge(gate_mm, 4 * n + j)
                    for q in range(4):
                        k = 4 * (j % 2) + q
                        last = V_.tensor_scalar(diag[:, q, :], IDENT[:], ADA[:, layer, 3 * sub + 2, k, j // 2:j // 2 + 1], None, ALU.mult)
                    last.then_inc(gate_diag, 1)

            def update_dve(n, Y):
                dve.wait_ge(ru_rstd, n + 1)
                dve.wait_ge(gate_ev, 4 * (n + 1))
                for t in range(NT):
                    chain.link(V_.scalar_tensor_tensor(Y[:, t, :], Y[:, t, :], RSTD[:, t:t + 1], GATE[:, t // NLAT, :], ALU.mult, ALU.mult))
                    V_.tensor_tensor(X[:, t, :], X[:, t, :], Y[:, t, :], ALU.add).then_inc(x_ready, 1)

            dve.wait_ge(const_ready, 9)
            norm_dve(0, 0, 0)

            def qx(h, t):
                for e in range(2):
                    last = V_.tensor_tensor(QX[:, t % 2, e], QT[:, :, t * P:(t + 1) * P],
                                            CROSS[:, e, t * P:(t + 1) * P].unsqueeze(1).to_broadcast([P, 2, P]), ALU.mult)
                last.then_inc(qx_ready, 1)

            def ret_head(h, first):
                if not first:
                    dve.wait_ge(y_mm, NT * h)
                chain.link(V_.tensor_scalar(DEC, DIFF, 0.0, LG[:, bass.ds(h, 1)], ALU.max, ALU.mult))
                chain.link(V_.tensor_scalar(DTMP, DIFF, 0.0, NLGB[:, bass.ds(h, 1)], ALU.min, ALU.mult))
                V_.tensor_tensor(DEC, DEC, DTMP, ALU.add).then_inc(te_ready, 1)
                dve.wait_ge(dec_ready, 5 * (h + 1))
                dve.wait_ge(qk_ev, 4 * (h + 1))
                for t in range(NLAT):
                    dve.wait_ge(sc_mm, NT * h + t + 1)
                    lo = 384 - P * t
                    V_.tensor_tensor(SC[:, t, :], ps[:, t, :], DEC[:, lo:lo + LAT], ALU.mult).then_inc(sc_ev, 1)
                dve.wait_ge(sc_mm, NT * (h + 1))
                V_.tensor_tensor(SCP, ps[:, 6, 0:P], DEC[:, 384:384 + P], ALU.mult).then_inc(sc_ev, 1)
                qx(h, 0)
                qx(h, 1)
                dve.wait_ge(kp_mm, h + 1)
                for e in range(2):
                    last = V_.tensor_scalar(KP[:, e, :], ps[:, 7, 0:DK], KDEC[:, e:e + 1], None, ALU.mult)
                last.then_inc(kp_ev, 1)
                for t in range(NT + 1):
                    if t < NT:
                        dve.wait_ge(y_mm, NT * h + t + 1)
                        chain.link(V_.bn_stats(BST, ps[:, t % 2, :]))
                        V_.memset(IDLE, 0.0)
                        V_.bn_aggr(MV[:, 2 * t:2 * t + 2], BST).then_inc(var_ready, 1)
                        dve.wait_ge(var_ready, NT * h + t + 1)
                        dve.wait_ge(silg, NT * h + t + 1)
                        if t >= 2 or not first:
                            dve.wait_ge(yt_mm, NT * h + t - 1 if t >= 2 else NT * h)
                        V_.scalar_tensor_tensor(YN[:, t % 2, :], ps[:, t % 2, :], MV[:, 2 * t:2 * t + 1], SILG[:, t % 2, :],
                                                ALU.subtract, ALU.mult).then_inc(yn_done, 1)
                        if t + 2 < NLAT:
                            qx(h, t + 2)
                    if t >= 1:
                        u = t - 1
                        dve.wait_ge(rsy_ready, NT * h + u + 1)
                        for half in range(2):
                            dve.wait_ge(out_mm, 2 * NT * h + 2 * u + half + 1)
                            dst = B1[:, u, half * HALF:(half + 1) * HALF]
                            if first:
                                V_.tensor_scalar(dst, ps[:, 6 + half, :], RSY[:, u:u + 1], None, ALU.mult).then_inc(out_acc, 1)
                            else:
                                V_.scalar_tensor_tensor(dst, ps[:, 6 + half, :], RSY[:, u:u + 1], dst, ALU.mult, ALU.add).then_inc(out_acc, 1)

            ret_head(0, True)
            with dve.Fori(1, HEADS) as h:
                chain.enter(h, 1, 2 + NT)
                ret_head(h, False)
            chain.leave(HEADS - 1)
            dve.wait_ge(yt_mm, NT * HEADS)
            gates_dve(0, 0, 0, YT[:, 0])
            update_dve(0, B1)

            def mix_dve(layer):
                b = {n: layer * v for n, v in per_layer.items()}
                n = 2 * layer + 1
                norm_dve(n, layer, 1)
                logits = ps[:, 0, 0:NT * NE].rearrange("p (t e) -> p t e", t=NT)
                dve.wait_ge(MS_["lg_mm"], b["lg_mm"] + 1)
                chain.link(V_.tensor_reduce(MX, logits, AX, ALU.max))
                V_.tensor_tensor(LGS, logits, MX.unsqueeze(2).to_broadcast([P, NT, NE]), ALU.subtract).then_inc(MS_["lgs"], 1)
                dve.wait_ge(MS_["ex"], b["ex"] + 1)
                chain.link(V_.tensor_reduce(RC, LGS, AX, ALU.add))
                chain.link(V_.reciprocal(RC, RC))
                V_.tensor_tensor(AFF, LGS, RC.unsqueeze(2).to_broadcast([P, NT, NE]), ALU.mult).then_inc(MS_["aff"], 1)
                dve.wait_ge(MS_["afft"], b["afft"] + 1)
                V_.tensor_copy(WK[0:NE, 0:LAT], ps[0:NE, 1, :])
                chain.link(V_.tensor_copy(WK[0:NE, LAT:TOK], ps[0:NE, 2, 0:P]))
                for lo, hi, cap in ((0, LAT, CAP), (LAT, TOK, CAPP)):
                    for _ in range(cap // 8):
                        chain.link(V_.max(M8[0:NE], WK[0:NE, lo:hi]))
                        chain.link(V_.match_replace(WK[0:NE, lo:hi], M8[0:NE], WK[0:NE, lo:hi], -1.0))
                chain.link(V_.tensor_scalar(SEL[0:NE], WK[0:NE], 0.0, None, ALU.is_lt))
                V_.tensor_tensor_scan(POS[0:NE, 0:LAT], SEL[0:NE, 0:LAT], SEL[0:NE, 0:LAT], 0.0, ALU.add, ALU.max)
                chain.link(V_.tensor_tensor_scan(POS[0:NE, LAT:TOK], SEL[0:NE, LAT:TOK], SEL[0:NE, LAT:TOK], 0.0, ALU.add, ALU.max))
                chain.link(V_.tensor_tensor(POS[0:NE], POS[0:NE], SEL[0:NE], ALU.mult))
                V_.memset(YEP, 0.0).then_inc(MS_["aff"], 1)
                dve.wait_ge(MS_["pos_tr"], b["pos_tr"] + 1)
                V_.tensor_copy(POST, ps[:, 3, 0:NT * NE].rearrange("p (t e) -> p t e", t=NT)).then_inc(MS_["post"], 1)
                dve.wait_ge(MS_["post"], b["post"] + 1)

                def one_hot(out, pair):
                    return V_.tensor_tensor(out, SLOTNO[:].unsqueeze(1).unsqueeze(1).to_broadcast([P, NT, 2, CAP]),
                                            POST[:, :, bass.ds(2 * pair, 2)].unsqueeze(3).to_broadcast([P, NT, 2, CAP]), ALU.is_equal)

                def gather_rows(pair):
                    one_hot(OH, pair).then_inc(MS_["oh"], 1)

                def gated_rows(pair):
                    chain.link(one_hot(OHG, pair))
                    V_.tensor_tensor(OHG, OHG, AFF[:, :, bass.ds(2 * pair, 2)].unsqueeze(3).to_broadcast([P, NT, 2, CAP]),
                                     ALU.mult).then_inc(MS_["ohg"], 1)

                def modulated(pair, u):
                    for half in range(2):
                        dve.wait_ge(MS_["xt_mm"], b["xt_mm"] + 4 * pair + 2 * u + half + 1)
                        for q in range(4):
                            k = 4 * half + q
                            src = ps[:, 6 + half, q * P:(q + 1) * P].rearrange("p (e r) -> p e r", e=2)
                            dst, src = (XET[:, :, k, 0:CAP], src) if u == 0 else (XET[:, :, k, CAP:ROWS], src[:, :, 0:CAPP])
                            last = V_.tensor_scalar(dst, src, scale_col(layer, 1, k, u), shift_col(layer, 1, k, u), ALU.mult, ALU.add)
                        last.then_inc(MS_["xt_ev"], 1)

                def hidden(e):
                    dve.wait_ge(MS_["sil"], b["sil"] + e + 1)
                    hid = HID[0:ROWS, :].rearrange("p (a n) -> p a n", a=2)
                    V_.tensor_tensor(hid, hid, ps[0:ROWS, 2:4, :], ALU.mult).then_inc(MS_["h"], 1)

                def accumulate(pair):
                    for t in range(NT):
                        for half in range(2):
                            dve.wait_ge(MS_["c_mm"], b["c_mm"] + 10 * pair + 2 * t + half + 1)
                            dst = YB2[:, t, half * HALF:(half + 1) * HALF]
                            V_.tensor_tensor(dst, ps[:, 6 + half, :], dst, ALU.add).then_inc(MS_["c_ev"], 1)

                gather_rows(0)
                modulated(0, 0)
                modulated(0, 1)
                dve.wait_ge(MS_["zero"], b["zero"] + 1)

                def turn(p, first, last):
                    if not first:
                        gated_rows(p - 1)
                    hidden(2 * p)
                    if not first:
                        accumulate(p - 1)
                    if not last:
                        gather_rows(p + 1)
                    hidden(2 * p + 1)
                    if not last:
                        modulated(p + 1, 0)
                        modulated(p + 1, 1)

                turn(0, True, False)
                with dve.Fori(1, PAIRS - 1) as p:
                    chain.enter(p, 1, 1)
                    turn(p, False, False)
                chain.leave(PAIRS - 2)
                turn(PAIRS - 1, False, True)
                gated_rows(PAIRS - 1)
                accumulate(PAIRS - 1)
                gates_dve(n, layer, 1, HID.rearrange("p (q n) -> p q n", q=8)[:, 0:4, :])
                update_dve(n, YB2)

            def rotate(x, cos, sin, ra, rb, dims):
                V_.tensor_tensor(ra, x, cos, ALU.mult)
                q = lambda v, i: v.rearrange("p g (b q r) -> p g b q r", b=2, q=2)[:, :, :, i]
                for i in range(2):
                    last = V_.tensor_tensor(q(rb, i), q(x, 1 - i), q(sin, i), ALU.mult)
                chain.link(last)
                return V_.tensor_tensor(x, ra, rb, ALU.add)

            def mla_dve():
                norm_dve(2, 1, 0)
                dve.wait_ge(cs_in, 16)
                dve.wait_ge(MA["ctx_in"], 64)
                dve.wait_ge(MA["lat_rstd"], 2)
                for t in range(NT):
                    for j, (lo, hi) in enumerate(((0, QL), (QL, QL + KVL))):
                        last = V_.tensor_scalar(LATN[:, t, lo:hi], LATN[:, t, lo:hi], LRS[:, j * NT + t:j * NT + t + 1], None, ALU.mult)
                    last.then_inc(MA["lat_n"], 1)
                dve.wait_ge(MA["lat_n"], NT)
                V_.tensor_tensor(CKO, LATN[:, NLAT, QL:QL + KVL], KVG, ALU.mult).then_inc(MA["cko"], 1)
                k = LATN[:, 0:NLAT, QL + KVL:WIN]
                ra = RA[:, 0:NLAT * ROPE].rearrange("p (t r) -> p t r", t=NLAT)
                rb = RB[:, 0:NLAT * ROPE].rearrange("p (t r) -> p t r", t=NLAT)
                chain.link(rotate(k, CS[:, 0], CS[:, 1], ra, rb, None))
                for j in range(2):
                    last = V_.tensor_copy(KRD[:, 1:NK, j * ROPE:(j + 1) * ROPE], LATN[:, :, QL + KVL:WIN])
                last.then_inc(MA["kr_ready"], 1)
                for t in range(NT):
                    dve.wait_ge(MA["ql_tr"], t + 1)
                    for c in range(3):
                        last = V_.tensor_scalar(QLT[:, c, t * P:(t + 1) * P], ps[:, 4 + t % 2, c * P:(c + 1) * P], NCOL[:, QN + c:QN + c + 1], None, ALU.mult)
                    last.then_inc(MA["ql_ev"], 1)
                for t in range(NLAT):
                    dve.wait_ge(MA["qr_ev"], t + 1)
                    if t >= 1:
                        dve.wait_ge(MA["qr_rot"], t)
                    v = lambda y: y.rearrange("p (h r) -> p h r", h=MH)
                    rotate(v(QR[:, t, :]), CS[:, 0, t, :].unsqueeze(1).to_broadcast([P, MH, ROPE]),
                           CS[:, 1, t, :].unsqueeze(1).to_broadcast([P, MH, ROPE]), v(RA), v(RB), None).then_inc(MA["qr_rot"], 1)

                def scores_max(h, t):
                    n = NT * h + t
                    dve.wait_ge(MA["s_mm"], n + 1)
                    b = (4, 6, 4, 6, 4)[t]
                    width = LAT + P if t < NLAT else P
                    src = ps[:, b:b + 2, :].rearrange("p a n -> p (a n)")[:, 0:width]
                    chain.link(V_.tensor_reduce(RMX[:, n % 2:n % 2 + 1], src, AX, ALU.max))
                    V_.tensor_scalar(RNM[:, n % 2:n % 2 + 1], RMX[:, n % 2:n % 2 + 1], -ATT_SCALE, None, ALU.mult).then_inc(MA["nm"], 1)

                for h in range(MH):
                    scores_max(h, 0)
                    for t in range(NT):
                        if t + 1 < NT:
                            scores_max(h, t + 1)
                        n = NT * h + t
                        width = LAT + P if t < NLAT else P
                        dve.wait_ge(MA["e_done"], n + 1)
                        chain.link(V_.reciprocal(RRC[:, n % 2:n % 2 + 1], RSM[:, n % 2:n % 2 + 1]))
                        V_.tensor_scalar(PR[:, n % 2, 0:width], PR[:, n % 2, 0:width], RRC[:, n % 2:n % 2 + 1], None, ALU.mult).then_inc(MA["pr"], 1)
                    dve.wait_ge(MA["o_mm"], 2 * h + 1)
                    V_.tensor_copy(OT[:, h, 0:LAT], ps[:, 1, :]).then_inc(MA["o_ev"], 1)
                    dve.wait_ge(MA["o_mm"], 2 * h + 2)
                    V_.tensor_copy(OT[:, h, LAT:TOK], ps[:, 2, 0:P]).then_inc(MA["o_ev"], 1)
                gates_dve(2, 1, 0, KNT.rearrange("p b n -> p (b n)")[:, 0:HALF].rearrange("p (q n) -> p q n", q=4))
                update_dve(2, B1)

            if STAGE >= 2:
                mix_dve(0)
            if STAGE >= 3:
                mla_dve()
                mix_dve(1)

        @block.tensor
        def _(pe):
            T = nc.tensor

            def mm(out, lhsT, rhs, first, last):
                return T.matmul(out, lhsT, rhs, start=first, stop=last)

            def tr(out, in_, n=P):
                return T.transpose(out, in_, IDENT[0:n, 0:n])

            pe.wait_ge(const_ready, 4)
            pe.wait_ge(rows_in, 16 * 8)
            tr(ps[:, 0, 0:COLS], RAW[0:COLS, 0, :], COLS).then_inc(cols_tr, 1)
            tr(ps[:, 1, 0:48], RAW[0:48, 1, :], 48).then_inc(cols_tr, 1)
            tr(ps[:, 2, 0:48], RAW[0:48, 2, :], 48).then_inc(cols_tr, 1)
            pe.wait_ge(cond_ready, 1)
            pe.wait_ge(cols_ev, 4)
            cond = NCOL[:, COND:QN].rearrange("p (c k) -> p c k", c=2)

            def ada_columns(n):
                pe.wait_ge(ada_ev, n + 1)
                if n >= 2:
                    pe.wait_ge(ada_col, n - 1)
                for q in range(4):
                    last = tr(ps[:, 2 + n % 2, 2 * q:2 * q + 2], AROW[0:2, n % 2, q * P:(q + 1) * P], 2)
                last.then_inc(ada_tr, 1)

            for n in range(2 * ADA_CHUNKS):
                pe.wait_ge(w_in[n % 6], 16 * (n // 6 + 1))
                if n >= 2:
                    pe.wait_ge(ada_ev, n - 1)
                for k in range(KD):
                    last = mm(ps[0:2, n % 2, :], cond[:, :, k], W8[:, n % 6, k, :], k == 0, k == KD - 1)
                last.then_inc(ada_mm, 1)
                if n >= 1:
                    ada_columns(n - 1)
            ada_columns(2 * ADA_CHUNKS - 1)

            def norm_pe(n):
                for t in range(NT):
                    pe.wait_ge(nt_xn, NT * n + t + 1)
                    if t >= 2:
                        pe.wait_ge(nt_evd, NT * n + t - 1)
                        pe.wait_ge(nt_eva, NT * n + t - 1)
                    for k in range(KD):
                        last = tr(ps[:, 4 + 2 * (t % 2) + k // 4, (k % 4) * P:(k % 4 + 1) * P], B1[:, t, k * P:(k + 1) * P])
                        if k % 4 == 3:
                            last.then_inc(nt_tr, 1)
                pe.wait_ge(nt_evd, NT * (n + 1))
                pe.wait_ge(nt_eva, NT * (n + 1))

            def gates_pe(n, diag):
                for j in range(4):
                    pe.wait_ge(gate_diag, 4 * n + j + 1)
                    mm(ps[:, j, :], ONES[:], diag, True, True).then_inc(gate_mm, 1)

            norm_pe(0)

            def ret_head(h, first):
                pe.wait_ge(w_in[0], 16 * RET0 + 32 * (h + 1))
                if not first:
                    pe.wait_ge(st_ev, 4 * h)
                for u in range(4):
                    if u >= 2:
                        pe.wait_ge(qk_ev, 4 * h + u - 1)
                    b, w, m = 2 * (u % 2), u // 2, u % 2
                    for k in range(KD):
                        mm(ps[:, b, :], WQK[:, w, k, m * P:(m + 1) * P], HT[:, k, 0:LAT], k == 0, k == KD - 1)
                    for k in range(KD):
                        last = mm(ps[:, b + 1, 0:P], WQK[:, w, k, m * P:(m + 1) * P], HT[:, k, LAT:TOK], k == 0, k == KD - 1)
                    last.then_inc(qk_mm, 1)
                pe.wait_ge(w_in[1], 16 * (RET0 + 1) + 16 * h)
                if not first:
                    pe.wait_ge(yt_ev, NT * h)
                for t in range(NT):
                    if t >= 2:
                        pe.wait_ge(v_ev, NT * h + t - 1)
                    for k in range(KD):
                        last = mm(ps[:, 4 + t % 2, :], HT[:, k, t * P:(t + 1) * P], W8[:, 1, k, :], k == 0, k == KD - 1)
                    last.then_inc(v_mm, 1)
                pe.wait_ge(qk_ev, 4 * (h + 1))
                for t in range(NLAT):
                    for m in range(2):
                        last = mm(ps[:, t, :], KT[:, m, t * P:(t + 1) * P], QT[:, m, 0:LAT], m == 0, m == 1)
                    last.then_inc(sc_mm, 1)
                if not first:
                    pe.wait_ge(out_acc, 2 * NT * h)
                for m in range(2):
                    last = mm(ps[:, 6, 0:P], KT[:, m, LAT:TOK], QT[:, m, LAT:TOK], m == 0, m == 1)
                last.then_inc(sc_mm, 1)
                for m in range(2):
                    last = tr(ps[:, 7, m * P:(m + 1) * P], KT[:, m, LAT:TOK])
                last.then_inc(kp_mm, 1)
                pe.wait_ge(w_in[2], 16 * (RET0 + 1) + 16 * h)
                pe.wait_ge(w_in[3], 16 * (RET0 + 1) + 16 * h)
                pe.wait_ge(s0_in, 32 * (h + 1))
                pe.wait_ge(v_ev, NT * (h + 1))
                pe.wait_ge(sc_ev, NT * (h + 1))
                for t in range(NT + 1):
                    if t < NT:
                        if t >= 2:
                            pe.wait_ge(yn_done, NT * h + t - 1)
                        if t < NLAT:
                            pe.wait_ge(qx_ready, NLAT * h + t + 1)
                            for j in range(NLAT):
                                mm(ps[:, t % 2, :], SC[:, j, t * P:(t + 1) * P], V[:, j, :], j == 0, False)
                            for j in range(4):
                                last = mm(ps[:, t % 2, :], QX[:, t % 2, j // 2, j % 2, :], S0[:, j // 2, j % 2, :], False, j == 3)
                        else:
                            last = mm(ps[:, t % 2, :], SCP, V[:, NLAT, :], True, True)
                        last.then_inc(y_mm, 1)
                    if t >= 1:
                        u = t - 1
                        pe.wait_ge(yn_done, NT * h + u + 1)
                        if u >= 2:
                            pe.wait_ge(yt_ev, NT * h + u - 1)
                        for c in range(4):
                            last = tr(ps[:, 4 + u % 2, c * P:(c + 1) * P], YN[:, u % 2, c * P:(c + 1) * P])
                        last.then_inc(yt_mm, 1)
                    if t < NT:
                        if t >= 2:
                            pe.wait_ge(silg, NT * h + t - 1)
                        for k in range(KD):
                            last = mm(ps[:, 2 + t % 2, :], HT[:, k, t * P:(t + 1) * P], W8[:, 2, k, :], k == 0, k == KD - 1)
                        last.then_inc(g_mm, 1)
                    if t >= 1:
                        pe.wait_ge(yt_ev, NT * h + u + 1)
                        if u == 0:
                            pe.wait_ge(kp_ev, h + 1)
                        else:
                            pe.wait_ge(out_acc, 2 * NT * h + 2 * u)
                        for half in range(2):
                            for c in range(4):
                                last = mm(ps[:, 6 + half, :], YT[:, u % 2, c, :], W4[:, 3, c, half * HALF:(half + 1) * HALF], c == 0, c == 3)
                            last.then_inc(out_mm, 1)
                pe.wait_ge(yn_done, NT * (h + 1))
                pe.wait_ge(silg, NT * (h + 1))
                for j in range(4):
                    mm(ps[:, j, :], KP[:, j // 2, (j % 2) * P:(j % 2 + 1) * P], V[:, NLAT, :], True, True).then_inc(st_mm, 1)

            ret_head(0, True)
            with pe.Fori(1, HEADS) as h:
                ret_head(h, False)
            pe.wait_ge(st_ev, 4 * HEADS)
            gates_pe(0, YT[:, 0])

            def mix_pe(layer):
                b = {n: layer * v for n, v in per_layer.items()}
                base = [16 * x for x in BEFORE_MIX[layer]]
                pe.wait_ge(gate_ev, 4 * (2 * layer + 1))
                norm_pe(2 * layer + 1)
                pe.wait_ge(wr_in, 16 * (layer + 1))
                for t in range(NT):
                    for k in range(KD):
                        last = mm(ps[:, 0, t * NE:(t + 1) * NE], HT[:, k, t * P:(t + 1) * P], WR[:, k, :], k == 0, k == KD - 1)
                last.then_inc(MS_["lg_mm"], 1)
                pe.wait_ge(MS_["aff"], 2 * b["aff"] + 1)
                for t in range(NT):
                    last = tr(ps[0:NE, 1 + t // 4, (t % 4) * P:(t % 4 + 1) * P], AFF[:, t, :])
                last.then_inc(MS_["afft"], 1)
                pe.wait_ge(MS_["aff"], 2 * b["aff"] + 2)
                for t in range(NT):
                    last = tr(ps[:, 3, t * NE:(t + 1) * NE], POS[0:NE, t * P:(t + 1) * P], NE)
                last.then_inc(MS_["pos_tr"], 1)

                def gather(pair, u):
                    tiles = range(NLAT) if u == 0 else (NLAT,)
                    for half in range(2):
                        for t in tiles:
                            last = mm(ps[:, 6 + half, :], OH[:, t].rearrange("p e r -> p (e r)"), B1[:, t, half * HALF:(half + 1) * HALF],
                                      t == tiles[0], t == tiles[-1])
                        last.then_inc(MS_["x_mm"], 1)

                def gather_tr(pair, u):
                    for half in range(2):
                        pe.wait_ge(MS_["x_ev"], b["x_ev"] + 4 * pair + 2 * u + half + 1)
                        for q in range(4):
                            k = 4 * half + q
                            last = tr(ps[:, 6 + half, q * P:(q + 1) * P], (XE, XEP)[u][:, k * P:(k + 1) * P])
                        last.then_inc(MS_["xt_mm"], 1)

                def up(e, par, half):
                    for w in (0, 2):
                        pe.wait_ge(w_in[w + half], base[w + half] + 16 * (e + 1))
                    for k in range(4):
                        for w in (0, 2):
                            for n in range(2):
                                kk = 4 * half + k
                                last = mm(ps[0:ROWS, w + n, :], XET[:, par, kk, :], W4[:, w + half, k, n * HALF:(n + 1) * HALF],
                                          kk == 0, kk == KD - 1)
                    last.then_inc(MS_[("ga_mm", "gb_mm")[half]], 1)

                def down(e):
                    for half in range(2):
                        pe.wait_ge(w_in[4 + half], base[4 + half] + 16 * (e + 1))
                        for k in range(4):
                            for n in range(2):
                                kk = 4 * half + k
                                last = mm(ps[0:ROWS, 4 + n, :], HTE[:, kk, :], W4[:, 4 + half, k, n * HALF:(n + 1) * HALF],
                                          kk == 0, kk == KD - 1)
                        last.then_inc(MS_[("da_mm", "db_mm")[half]], 1)

                def hidden_tr(e):
                    pe.wait_ge(MS_["h"], b["h"] + e + 1)
                    for c in range(KD):
                        last = tr(ps[:, 6 + c // 4, (c % 4) * ROWS:(c % 4 + 1) * ROWS], HID[0:ROWS, c * P:(c + 1) * P], ROWS)
                        if c % 4 == 3:
                            last.then_inc(MS_["t_mm"], 1)

                def combine_tr(pair):
                    pe.wait_ge(MS_["ohg"], b["ohg"] + pair + 1)
                    for t in range(NT):
                        last = tr(ps[:, 6 + t // 4, (t % 4) * P:(t % 4 + 1) * P], OHG[:, t].rearrange("p e r -> p (e r)"))
                        if t >= 3:
                            last.then_inc(MS_["ct_mm"], 1)

                def combine(pair):
                    pe.wait_ge(MS_["ct_ev"], b["ct_ev"] + 2 * (pair + 1))
                    pe.wait_ge(MS_["y_ev"], b["y_ev"] + 2 * (pair + 1))
                    for t in range(NT):
                        for half in range(2):
                            if t >= 1:
                                pe.wait_ge(MS_["c_ev"], b["c_ev"] + 10 * pair + 2 * t + half - 1)
                            mm(ps[:, 6 + half, :], CT[:, t, :], (YE if t < NLAT else YEP)[:, half * HALF:(half + 1) * HALF],
                               True, True).then_inc(MS_["c_mm"], 1)

                pe.wait_ge(MS_["oh"], b["oh"] + 1)
                gather(0, 0)
                pe.wait_ge(MS_["x_ev"], b["x_ev"] + 2)
                gather(0, 1)
                pe.wait_ge(MS_["x_ev"], b["x_ev"] + 4)
                gather_tr(0, 0)
                pe.wait_ge(MS_["xt_ev"], b["xt_ev"] + 2)
                gather_tr(0, 1)
                pe.wait_ge(MS_["xt_ev"], b["xt_ev"] + 4)

                def turn(p, first, last):
                    if not first:
                        pe.wait_ge(MS_["xt_ev"], b["xt_ev"] + 4 * (p + 1))
                        pe.wait_ge(MS_["h"], b["h"] + 2 * p)
                    up(2 * p, 0, 0)
                    up(2 * p, 0, 1)
                    if not first:
                        pe.wait_ge(MS_["t_ev"], b["t_ev"] + 4 * p)
                        pe.wait_ge(MS_["y_ev"], b["y_ev"] + 2 * p - 1)
                        down(2 * p - 1)
                    hidden_tr(2 * p)
                    pe.wait_ge(MS_["t_ev"], b["t_ev"] + 4 * p + 2)
                    if not first:
                        combine_tr(p - 1)
                        combine(p - 1)
                    up(2 * p + 1, 1, 0)
                    if not last:
                        if not first:
                            pe.wait_ge(MS_["c_ev"], b["c_ev"] + 10 * p)
                        pe.wait_ge(MS_["oh"], b["oh"] + p + 2)
                        gather(p + 1, 0)
                    up(2 * p + 1, 1, 1)
                    if not last:
                        pe.wait_ge(MS_["x_ev"], b["x_ev"] + 4 * (p + 1) + 2)
                        gather(p + 1, 1)
                    if not first:
                        pe.wait_ge(MS_["y_ev"], b["y_ev"] + 2 * p)
                    down(2 * p)
                    if not last:
                        pe.wait_ge(MS_["x_ev"], b["x_ev"] + 4 * (p + 2))
                        gather_tr(p + 1, 0)
                        pe.wait_ge(MS_["xt_ev"], b["xt_ev"] + 4 * (p + 1) + 2)
                    elif True:
                        pe.wait_ge(MS_["c_ev"], b["c_ev"] + 10 * p)
                    hidden_tr(2 * p + 1)
                    pe.wait_ge(MS_["t_ev"], b["t_ev"] + 4 * (p + 1))
                    if not last:
                        gather_tr(p + 1, 1)

                turn(0, True, False)
                with pe.Fori(1, PAIRS - 1) as p:
                    turn(p, False, False)
                turn(PAIRS - 1, False, True)
                pe.wait_ge(MS_["y_ev"], b["y_ev"] + NE - 1)
                down(NE - 1)
                combine_tr(PAIRS - 1)
                combine(PAIRS - 1)
                gates_pe(2 * layer + 1, HID[:, 0:HALF])

            def mla_pe():
                pe.wait_ge(gate_ev, 8)
                norm_pe(2)
                base = [16 * n for n in BEFORE_MLA]
                for s in range(2):
                    pe.wait_ge(w_in[s], base[s] + 16)
                for t in range(NT):
                    if t >= 2:
                        pe.wait_ge(MA["lat_ev"], t - 1)
                    b = 2 * (t % 2)
                    for n, (lo, hi) in enumerate(((0, HALF), (HALF, WIN))):
                        for k in range(KD):
                            last = mm(ps[:, b + n, 0:hi - lo], HT[:, k, t * P:(t + 1) * P], WIN2[k // 4][:, k % 4, lo:hi], k == 0, k == KD - 1)
                    last.then_inc(MA["lat_mm"], 1)
                for t in range(NT):
                    pe.wait_ge(MA["lat_n"], t + 1)
                    if t >= 2:
                        pe.wait_ge(MA["ql_ev"], t - 1)
                    for c in range(3):
                        last = tr(ps[:, 4 + t % 2, c * P:(c + 1) * P], LATN[:, t, c * P:(c + 1) * P])
                    last.then_inc(MA["ql_tr"], 1)
                pe.wait_ge(MA["kr_ready"], 1)
                for kt in range(NK):
                    if kt >= 2:
                        pe.wait_ge(MA["kv_ev"], kt - 1)
                    for c in range(2):
                        src = CKC[:, c * P:(c + 1) * P] if kt == 0 else LATN[:, kt - 1, QL + c * P:QL + (c + 1) * P]
                        tr(ps[:, 6 + kt % 2, c * P:(c + 1) * P], src)
                    tr(ps[:, 6 + kt % 2, 2 * P:3 * P], KRD[:, kt, :]).then_inc(MA["kv_tr"], 1)
                pe.wait_ge(MA["ql_ev"], NT)
                for s in (2, 3):
                    pe.wait_ge(w_in[s], base[s] + 16)
                for t in range(NT):
                    if t == 4:
                        pe.wait_ge(MA["qr_ev"], 1)
                    for g in range(2):
                        for c in range(3):
                            last = mm(ps[:, t % 4, g * 256:(g + 1) * 256], QLT[:, c, t * P:(t + 1) * P], WQB[g][:, c, :, P:P + ROPE], c == 0, c == 2)
                    last.then_inc(MA["qr_mm"], 1)
                pe.wait_ge(w_in[0], base[0] + 32)
                pe.wait_ge(MA["kv_ev"], NK)
                for kt in range(NK):
                    for half in range(2):
                        if kt >= 1:
                            pe.wait_ge(MA["vv_ev"], 2 * kt + half - 1)
                        for c in range(2):
                            last = mm(ps[:, 6 + half, :], KVT[:, c, kt * P:(kt + 1) * P], WKV[:, c, 4 * half:4 * half + 4, P:2 * P], c == 0, c == 1)
                        last.then_inc(MA["vv_mm"], 1)
                for t in range(NT):
                    pe.wait_ge(*((MA["qr_rot"], t + 1) if t < NLAT else (MA["qr_ev"], NT)))
                    if t >= 2:
                        pe.wait_ge(MA["qrt_ev"], t - 1)
                    for c in range(4):
                        last = tr(ps[:, 4 + t % 2, c * P:(c + 1) * P], QR[:, t, c * P:(c + 1) * P])
                    last.then_inc(MA["qrt_tr"], 1)
                pe.wait_ge(MA["qrt_ev"], NT)
                pe.wait_ge(MA["vv_ev"], 2 * NK)

                def scores(h, t):
                    n = NT * h + t
                    if t >= 2:
                        pe.wait_ge(MA["e_done"], n - 1)
                    elif h:
                        pe.wait_ge(MA["e_done"], NT * h)
                    b = (4, 6, 4, 6, 4)[t]
                    r = ROPE * (h % 2)
                    for lo, hi in (((0, HALF), (HALF, LAT + P)) if t < NLAT else ((LAT + P, NK * P),)):
                        mm(ps[:, b, 0:hi - lo], QNT[:, h % 2, t * P:(t + 1) * P], KNT[:, h % 2, lo:hi], True, False)
                        last = mm(ps[:, b, 0:hi - lo], QRT[r:r + ROPE, h // 2, t * P:(t + 1) * P], KRT[r:r + ROPE, lo:hi], False, True)
                        b += 1
                    last.then_inc(MA["s_mm"], 1)

                for h in range(MH):
                    if h:
                        pe.wait_ge(MA["pt_ev"], NT * h)
                        pe.wait_ge(MA["o_ev"], 2 * h)
                    for n, (lo, hi) in enumerate(((0, HALF), (HALF, NK * P))):
                        for c in range(2):
                            last = mm(ps[:, n, 0:hi - lo], WKV[:, c, h, 0:P], KVT[:, c, lo:hi], c == 0, c == 1)
                    last.then_inc(MA["kn_mm"], 1)
                    for n, (lo, hi) in enumerate(((0, HALF), (HALF, TOK))):
                        for c in range(3):
                            last = mm(ps[:, 2 + n, 0:hi - lo], WQB[h // 4][:, c, h % 4, 0:P], QLT[:, c, lo:hi], c == 0, c == 2)
                    last.then_inc(MA["kn_mm"], 1)
                    pe.wait_ge(MA["kn_ev"], 2 * (h + 1))
                    scores(h, 0)
                    for t in range(NT):
                        if t + 1 < NT:
                            scores(h, t + 1)
                        n = NT * h + t
                        pe.wait_ge(MA["pr"], n + 1)
                        if t >= 2:
                            pe.wait_ge(MA["pt_ev"], n - 1)
                        b = 2 * (t % 2)
                        for kt in range(NT if t < NLAT else 1):
                            last = tr(ps[:, b + kt // 4, (kt % 4) * P:(kt % 4 + 1) * P], PR[:, n % 2, kt * P:(kt + 1) * P])
                        last.then_inc(MA["pt_tr"], 1)
                    pe.wait_ge(MA["pt_ev"], NT * (h + 1))
                    for kt in range(NT):
                        last = mm(ps[:, 1, :], B1[:, kt, h * P:(h + 1) * P], PT[:, kt, :], kt == 0, kt == NT - 1)
                    last.then_inc(MA["o_mm"], 1)
                    mm(ps[:, 2, 0:P], VP[:, h * P:(h + 1) * P], PTP, True, True).then_inc(MA["o_mm"], 1)
                pe.wait_ge(w_in[1], base[1] + 32)
                pe.wait_ge(w_in[2], base[2] + 32)
                pe.wait_ge(MA["o_ev"], 2 * MH)
                for t in range(NT):
                    for half in range(2):
                        if t >= 2:
                            pe.wait_ge(MA["mo_ev"], 2 * (t - 2) + half + 1)
                        for k in range(MH):
                            last = mm(ps[:, 4 + 2 * (t % 2) + half, :], OT[:, k, t * P:(t + 1) * P], W4[:, 1 + k // 4, k % 4, half * HALF:(half + 1) * HALF],
                                      k == 0, k == MH - 1)
                        last.then_inc(MA["mo_mm"], 1)
                gates_pe(2, KNT.rearrange("p b n -> p (b n)")[:, 0:HALF])

            if STAGE >= 2:
                mix_pe(0)
            if STAGE >= 3:
                mla_pe()
                mix_pe(1)


_INS = ["x_prompt", "x_sample", "state_ret_fwd", "state_ret_bwd", "cache_mla_ckv", "cache_mla_krope", "c", "c_ctx",
        "ada_w", "ada_b", "norm_pre", "norm_post", "ret_w_in", "ret_decay_fwd", "ret_decay_bwd", "ret_w_out",
        "mla_w_in", "mla_q_norm", "mla_kv_norm", "mla_w_q_b", "mla_w_kv_b", "mla_w_out",
        "moe_w_router", "moe_w_gate", "moe_w_up", "moe_w_down"]
_OUTS = [("y_prompt", (1, 128, 1024)), ("y_sample", (1, 512, 1024)), ("state_fwd", (1, 1, 4, 256, 512)),
         ("state_bwd", (1, 1, 4, 256, 512)), ("new_ckv", (1, 1, 128, 256)), ("new_krope", (1, 1, 128, 64))]


def rotary_tables():
    import numpy as np
    grid, half = 64, ROPE // 2
    row = np.repeat(np.arange(LAT // grid, dtype=np.float32), grid)
    col = np.tile(np.arange(grid, dtype=np.float32), LAT // grid)
    inv = (np.float32(1.0) / (np.float32(10000.0) ** (np.arange(0, half, 2, dtype=np.float32) / np.float32(half)))).astype(np.float32)
    ar, ac = row[:, None] * inv, col[:, None] * inv
    ang = np.concatenate([ar, ar, ac, ac], axis=-1).astype(np.float32)
    sign = np.repeat(np.array([-1, 1, -1, 1], np.float32), half // 2)
    return np.stack([np.cos(ang), np.sin(ang) * sign]).astype(np.float32)


STAGE = 3


def kernel(**inputs):
    import numpy as _np
    import concourse.bacc as _bacc
    from concourse import mybir as _mybir
    from concourse.bass_utils import run_bass_kernel_spmd as _run

    nc = _bacc.Bacc("TRN2", target_bir_lowering=False, num_devices=1)
    arrays, a, o = {}, {}, {}
    for name in _INS + ["rotary"]:
        x = rotary_tables() if name == "rotary" else _np.ascontiguousarray(inputs[name])
        arrays[f"in_{name}_dram"] = x
        a[name] = nc.dram_tensor(f"in_{name}_dram", x.shape, _mybir.dt.from_np(x.dtype), kind="ExternalInput").ap()
    for name, shape in _OUTS:
        o[name] = nc.dram_tensor(f"out_{name}_dram", shape, _mybir.dt.float32, kind="ExternalOutput").ap()
    trunk(nc, a, o, STAGE)
    r = _run(nc, [arrays], core_ids=[0])
    return tuple(r.results[0][f"out_{name}_dram"] for name, _ in _OUTS)
```

```python
from contextlib import ExitStack

import concourse.bass as bass
from concourse import mybir

F32 = mybir.dt.float32
F32R = mybir.dt.float32r
ALU = mybir.AluOpType
ACT = mybir.ActivationFunctionType
AX = mybir.AxisListType.X

P = 128
D = 1024
KD = D // P
NLAT = 4
NT = 5
LAT = NLAT * P
TOK = NT * P
DEPTH = 2
ADA_CHUNKS = 12
ADA_FIRST = 4
HALF = 512
SLOT = 4096
HEADS = 4
DK, DV = 256, 512
NE = 16
PAIRS = NE // 2
CAP = 64
CAPP = 16
ROWS = CAP + CAPP
MH = 8
QL, KVL, ROPE = 384, 256, 64
WIN = QL + KVL + ROPE
NK = 6
UNIT = 2048
UP, DOWN = 8, 4
PART = UNIT // 2
UNITS = NE * (UP + DOWN)
RAWS, SPLITS = 4, 6
AHEAD = SPLITS - 1
EPS = 1e-6
ATT_SCALE = float((128 + ROPE) ** -0.5)


class Chain:

    def __init__(self, eng, sem):
        self.eng, self.sem, self.base, self.n = eng, sem, 0, 0

    def link(self, ins):
        self.n += 1
        ins.then_inc(self.sem, 1)
        self.eng.wait_ge(self.sem, self.base + self.n)

    def enter(self, i, first, per):
        self.saved, self.per, self.turns_n = self.n, per, 0
        self.base, self.n = (i - first) * per + self.saved, 0

    def leave(self, turns):
        assert self.n == self.per, (self.n, self.per)
        self.base, self.n = 0, self.saved + turns * self.per


def trunk(nc, a, o, STAGE=9):
    ctx = ExitStack()
    with ctx:
        def sb(name, shape, stack=None, dt=F32):
            return (stack or ctx).enter_context(nc.sbuf_tensor(name, shape, dt))

        def sem(name):
            return ctx.enter_context(nc.semaphore(name))

        with ExitStack() as heads_memory:
            ADA_RAW = sb("ADA_RAW", [P, 2, D], heads_memory)
            ADA_HI = sb("ADA_HI", [P, 2, HALF], heads_memory, F32R)
            HEADS_BUF = sb("HEADS_BUF", [P, 2 * D], heads_memory)
        X = sb("X", [P, NT, D])
        B1 = sb("B1", [P, NT, D])
        B2 = sb("B2", [P, KD * TOK])
        GATE = sb("GATE", [P, 2, D])
        IDENT = sb("IDENT", [P, P])
        ONES = sb("ONES", [P, P])
        ADA = sb("ADA", [P, DEPTH, 6, KD, 2])
        NCOL = sb("NCOL", [P, 88])
        BCOL = sb("BCOL", [P, DEPTH, 48])
        CS = sb("CS", [P, 2, NLAT, ROPE])
        SLOTNO = sb("SLOTNO", [P, CAP])
        STEP1 = sb("STEP1", [P, LAT])
        COND_HL = sb("COND_HL", [P, KD, 4], dt=F32R)
        SMALL = sb("SMALL", [P, 144])
        with ExitStack() as mixer_memory:
            W = sb("W", [P, 6, SLOT], mixer_memory)
            REGION = sb("REGION", [P, 8960], mixer_memory)
        with ExitStack() as heads_memory:
            sb("OTHERS", [P, 6 * SLOT + 7552], heads_memory)
            ADA_LO = sb("ADA_LO", [P, 2, HALF], heads_memory, F32R)
        with ExitStack() as mixture_memory:
            RAW_W = sb("RAW_W", [P, RAWS, UNIT], mixture_memory)
            W_HI = sb("W_HI", [P, SPLITS, PART], mixture_memory, F32R)
            W_LO = sb("W_LO", [P, SPLITS, PART], mixture_memory, F32R)
            XET_HI = sb("XET_HI", [P, 2, KD, ROWS], mixture_memory, F32R)
            XET_LO = sb("XET_LO", [P, 2, KD, ROWS], mixture_memory, F32R)
            HTE_HI = sb("HTE_HI", [P, KD, ROWS], mixture_memory, F32R)
            HTE_LO = sb("HTE_LO", [P, KD, ROWS], mixture_memory, F32R)
            CT_HI = sb("CT_HI", [P, NT, P], mixture_memory, F32R)
            CT_LO = sb("CT_LO", [P, NT, P], mixture_memory, F32R)
            YE_HI = sb("YE_HI", [P, 2, D], mixture_memory, F32R)
            YE_LO = sb("YE_LO", [P, 2, D], mixture_memory, F32R)
            MIXREG = sb("MIXREG", [P, 3 * TOK], mixture_memory)

        HT = B2[:].rearrange("p (k t) -> p k t", k=KD)
        YB2 = B2[:].rearrange("p (t d) -> p t d", t=NT)
        ps = ctx.enter_context(nc.psum_tensor("ps", [P, 8, HALF], F32))

        small_at = [0]

        def small(n):
            small_at[0] += n
            assert small_at[0] <= 144
            return SMALL[:, small_at[0] - n:small_at[0]]

        SSN, MSN, RSTDN = small(NT), small(NT), small(NT)
        SSU, MSU, RSTDU = small(NT), small(NT), small(NT)
        NHALF = small(NT)
        LG = small(8)
        NLGB, LGB513 = small(4), small(4)
        LU, LV, LW = small(8), small(8), small(8)
        TPOS = small(2)
        KDEC = small(2)
        BST, MV, RV, RSY = small(6), small(2 * NT), small(NT), small(NT)
        EPSC, IDLE = small(1), small(1)

        def carve(tensor, width):
            at = [0]

            def take(*shape):
                n = 1
                for s in shape:
                    n *= s
                at[0] += n
                assert at[0] <= width, (at[0], width)
                view = tensor[:, at[0] - n:at[0]]
                if len(shape) == 2:
                    return view.rearrange("p (a b) -> p a b", a=shape[0])
                if len(shape) == 3:
                    return view.rearrange("p (a b c) -> p a b c", a=shape[0], b=shape[1])
                if len(shape) == 4:
                    return view.rearrange("p (a b c e) -> p a b c e", a=shape[0], b=shape[1], c=shape[2])
                return view
            return take

        take = carve(REGION, 8960)
        RAW = take(3, P)
        AROW = take(2, HALF)
        take = carve(REGION, 7552)
        STATE = take(2, HALF)
        QT, KT = take(2, TOK), take(2, TOK)
        SILG = take(2, HALF)
        STATES = [STATE[:, 0, :], STATE[:, 1, :], SILG[:, 0, :], SILG[:, 1, :]]
        CROSS = take(2, LAT)
        YT = take(2, 4, P)
        DEC = take(896)
        WLAST = W[:].rearrange("p s n -> p (s n)")[:, 4 * SLOT:6 * SLOT]
        take = carve(WLAST, 2 * SLOT)
        V = take(NT, DV)
        SC = take(NLAT, LAT)
        SCP = take(P)
        S0 = take(2, 2, DV)
        KP = take(2, DK)
        DIFF = take(896)
        ROWS4 = YT.rearrange("p b c n -> p b (c n)")
        take = carve(HEADS_BUF[:], 2 * D)
        QX = take(2, 2, 2, P)
        YN = take(2, HALF)
        DTMP = QX.rearrange("p a b c e -> p (a b c e)")[:, 0:896]
        HID = MIXREG[:, 0:D]
        take = carve(GATE[:].rearrange("p c d -> p (c d)"), 2 * D)
        XET = take(2, KD, ROWS)
        OH = take(NT, 2, CAP)
        take = carve(STEP1, LAT)
        WR = take(KD, NE)
        AFF = take(NT, NE)
        POST = take(NT, NE)
        LGS = take(NT, NE)
        MX = take(NT)
        RC = take(NT)
        M8 = take(8)
        WK, SEL, POS = (MIXREG[:, i * TOK:(i + 1) * TOK] for i in range(3))

        take = carve(REGION, 8960)
        KVT = take(2, NK * P)
        KRT = take(NK * P)
        KNT = take(2, NK * P)
        QNT = take(2, TOK)
        VP = take(D)
        PR = take(2, LAT + P)
        PTP = take(P)
        KVG = take(KVL)
        CKC = take(KVL)
        LSS, LMS, LRS = take(2 * NT), take(2 * NT), take(2 * NT)
        RMX, RNM, RSM, RRC = take(2), take(2), take(2), take(2)
        KRD = KNT.rearrange("p b n -> p (b n)")[:, 0:NK * P].rearrange("p (t n) -> p t n", t=NK)
        RAB = QNT.rearrange("p b n -> p (b n)")[:, 0:2 * HALF].rearrange("p (j n) -> p j n", j=2)
        RA, RB = (QNT.rearrange("p b n -> p (b n)")[:, x * HALF:(x + 1) * HALF] for x in range(2))
        CKO = PR[:, 0, 0:KVL]
        take = carve(WLAST, 2 * SLOT)
        LATN = take(NT, WIN)
        QLT = take(3, TOK)
        QRT = take(4, TOK)
        QR = WLAST[:, 0:NT * HALF].rearrange("p (t n) -> p t n", t=NT)
        PT = WLAST[:, 0:NT * LAT].rearrange("p (t n) -> p t n", t=NT)
        OT = B2[:].rearrange("p (h t) -> p h t", h=MH)
        WIN2 = [W[:, s, 0:4 * WIN].rearrange("p (k n) -> p k n", k=4) for s in (0, 1)]
        WQB = [W[:, s, 0:3 * 768].rearrange("p (k h n) -> p k h n", k=3, h=4) for s in (2, 3)]
        WKV = W[:, 0, :].rearrange("p (k h n) -> p k h n", k=2, h=MH)

        rows_in, x_in, dec_in, cs_in = sem("rows_in"), sem("x_in"), sem("dec_in"), sem("cs_in")
        w_in = [sem(f"w_in{s}") for s in range(6)]
        const_ready = sem("const_ready")
        cols_tr, cols_ev = sem("cols_tr"), sem("cols_ev")
        cond_ready = sem("cond_ready")
        ada_mm, ada_ev, ada_tr, ada_col = sem("ada_mm"), sem("ada_ev"), sem("ada_tr"), sem("ada_col")
        ada_ready = sem("ada_ready")
        cond_hi, cond_lo, ada2_used, ada2_ev = sem("cond_hi"), sem("cond_lo"), sem("ada2_used"), sem("ada2_ev")
        ada2_in = [sem("ada2_in0"), sem("ada2_in1")]
        ada2_hi, ada2_lo, ada2_tr, ada2_col = sem("ada2_hi"), sem("ada2_lo"), sem("ada2_tr"), sem("ada2_col")
        x_back = sem("x_back")
        dve_chain, pool_chain = sem("dve_chain"), sem("pool_chain")
        nt_ss, nt_rstd, nt_xn, nt_tr = sem("nt_ss"), sem("nt_rstd"), sem("nt_xn"), sem("nt_tr")
        nt_evd, nt_eva = sem("nt_evd"), sem("nt_eva")
        gate_diag, gate_mm, gate_ev = sem("gate_diag"), sem("gate_mm"), sem("gate_ev")
        ru_ss, ru_rstd, x_ready = sem("ru_ss"), sem("ru_rstd"), sem("x_ready")
        stored = sem("stored")
        s0_in = sem("s0_in")
        lu_ready, lg_ready, te_ready, dec_ready = sem("lu_ready"), sem("lg_ready"), sem("te_ready"), sem("dec_ready")
        qk_mm, qk_ev, v_mm, v_ev = sem("qk_mm"), sem("qk_ev"), sem("v_mm"), sem("v_ev")
        sc_mm, sc_ev, kp_mm, kp_ev = sem("sc_mm"), sem("sc_ev"), sem("kp_mm"), sem("kp_ev")
        qx_ready, y_mm, g_mm, silg = sem("qx_ready"), sem("y_mm"), sem("g_mm"), sem("silg")
        var_ready, rsy_ready, yn_done = sem("var_ready"), sem("rsy_ready"), sem("yn_done")
        yt_mm, yt_ev, out_mm, out_acc = sem("yt_mm"), sem("yt_ev"), sem("out_mm"), sem("out_acc")
        st_mm, st_ev = sem("st_mm"), sem("st_ev")
        st_out = [sem(f"st_out{j}") for j in range(4)]

        MLAN = ("ctx_in", "lat_mm", "lat_ev", "lat_ss", "lat_rstd", "lat_n", "kr_ready", "cko", "new_out",
                "ql_tr", "ql_ev", "kv_tr", "kv_ev", "qr_mm", "qr_ev", "qr_rot", "qrt_tr", "qrt_ev", "vv_mm", "vv_ev",
                "kn_mm", "kn_ev", "s_mm", "nm", "e_done", "pr", "pt_tr", "pt_ev", "o_mm", "o_ev", "mo_mm", "mo_ev")
        MA = {n: sem("att_" + n) for n in MLAN}

        def act_copy(out, in_, scale=1.0):
            return nc.scalar.activation(out, in_, ACT.Copy, scale=scale)

        NPRE, NPOST, COND, QN, KVN = 0, 32, 64, 80, 83
        COLS = 85

        def norm_col(kind, layer, sub):
            at = (NPRE if kind == "pre" else NPOST) + (layer * 2 + sub) * KD
            return NCOL[:, at:at + KD]

        def scale_col(layer, sub, k, c):
            return ADA[:, layer, 3 * sub + 1, k, c:c + 1]

        def shift_col(layer, sub, k, c):
            return ADA[:, layer, 3 * sub, k, c:c + 1]

        MIXN = ("lg_mm", "lt_ev", "lgt", "lgs", "ex", "aff", "afft", "pos_tr", "post", "oh", "ohg",
                "hi", "lo", "used", "xh", "xl", "t_lo", "y_lo", "ct_lo", "sil", "h", "t_mm", "t_ev", "y_ev",
                "ct_mm", "ct_ev", "c_mm", "c_ev", "x_mm", "xt_ev", "zero")
        MS_ = {n: sem("mix_" + n) for n in MIXN}
        wr_in = sem("wr_in")
        raw_in = [sem(f"raw_in{s}") for s in range(RAWS)]

        def first_unit(p, first):
            return (0, 0) if first else (24 * p - 4, 20)

        def first_part(p, first):
            base, place = first_unit(p, first)
            return 2 * base, 2 * place

        def turn_units(p, first):
            up = lambda e: [(e, w, q) for q in range(4) for w in range(2)]
            down = lambda e: [(e, 2, q) for q in range(4)]
            return up(0) + up(1) + down(0) if first else up(2 * p) + down(2 * p - 1) + up(2 * p + 1) + down(2 * p)

        def turn_parts(first):
            return (2 * UP, 2 * UP, 4 * UP, 4 * UP + 2 * DOWN) if first else (2 * UP, 2 * UP + 2 * DOWN, 4 * UP + 2 * DOWN, 4 * UP + 4 * DOWN)
        per_layer = dict(lg_mm=1, lt_ev=1, lgt=1, lgs=1, ex=1, aff=1, afft=1, pos_tr=1, post=1, oh=PAIRS, ohg=PAIRS,
                         hi=2 * UNITS, lo=2 * UNITS, used=2 * UNITS, xh=2 * PAIRS, xl=2 * PAIRS, t_lo=2 * NE, y_lo=NE, ct_lo=2 * PAIRS, sil=NE, h=NE, t_mm=2 * NE,
                         t_ev=2 * NE, y_ev=NE, ct_mm=2 * PAIRS, ct_ev=2 * PAIRS, c_mm=10 * PAIRS,
                         c_ev=10 * PAIRS, x_mm=3 * PAIRS, xt_ev=3 * PAIRS, zero=1)

        ADA_TILES = [(0, 2, 4), (0, 2, 5), (1, 3, 0), (1, 3, 1), (1, 3, 2)]

        def ada2_chunk(h, t):
            _, step, at = ADA_TILES[t]
            return step * h + at

        ada_w = a["ada_w"].rearrange("l (k p) n -> l p k n", p=P)
        ret_in = a["ret_w_in"][0].rearrange("(k p) n -> p k n", p=P)
        ret_out = a["ret_w_out"][0].rearrange("(h c p) n -> h p c n", p=P, c=4)
        W8 = W[:].rearrange("p s (k n) -> p s k n", k=KD)
        W4 = W[:].rearrange("p s (k n) -> p s k n", k=4)
        WQK = W[:, 0, :].rearrange("p (w k n) -> p w k n", w=2, k=KD)

        ADA_LOADS = [0, 0, 1, 1, 1, 1]
        MLA_LOADS = [2, 2, 2, 1, 0, 0]
        BEFORE_MIX = [[n + m for n, m in zip(ADA_LOADS, (2 * HEADS, HEADS, HEADS, HEADS, 0, 0))]]
        BEFORE_MLA = BEFORE_MIX[0]
        BEFORE_MIX.append([n + m for n, m in zip(BEFORE_MLA, MLA_LOADS)])

        block = ctx.enter_context(nc.Block())

        @block.sync
        def _(sp):
            for e, w in enumerate(("ret_decay_fwd", "ret_decay_bwd")):
                sp.dma_start(LU[:, 4 * e:4 * e + 4], a[w].to_broadcast([P, 4])).then_inc(dec_in, 16)
            sp.dma_start(RAW[0:32, 0, :], a["norm_pre"].rearrange("l s (k p) -> (l s k) p", p=P)).then_inc(rows_in, 16)
            sp.dma_start(RAW[32:64, 0, :], a["norm_post"].rearrange("l s (k p) -> (l s k) p", p=P)).then_inc(rows_in, 16)
            sp.dma_start(RAW[64:72, 0, :], a["c"].rearrange("b (k p) -> (b k) p", p=P)).then_inc(rows_in, 16)
            sp.dma_start(RAW[72:80, 0, :], a["c_ctx"].rearrange("(k p) -> k p", p=P)).then_inc(rows_in, 16)
            sp.dma_start(W8[:, 2], ada_w[0, :, :, 0:HALF]).then_inc(w_in[2], 16)
            sp.dma_start(RAW[80:83, 0, :], a["mla_q_norm"].rearrange("l (k p) -> (l k) p", p=P)).then_inc(rows_in, 16)
            sp.dma_start(RAW[83:85, 0, :], a["mla_kv_norm"].rearrange("l (k p) -> (l k) p", p=P)).then_inc(rows_in, 16)
            for layer in range(DEPTH):
                sp.dma_start(RAW[0:48, 1 + layer, :], a["ada_b"][layer].rearrange("(k p) -> k p", p=P)).then_inc(rows_in, 16)
            for n in range(1, ADA_FIRST):
                sp.dma_start(W8[:, 2 + n], ada_w[0, :, :, n * HALF:(n + 1) * HALF]).then_inc(w_in[2 + n], 16)
                if n == 2:
                    sp.dma_start(X[:, 0:NLAT, :], a["x_sample"][0].rearrange("(t p) d -> p t d", p=P)).then_inc(x_in, 16)
                    sp.dma_start(X[:, NLAT, :], a["x_prompt"][0]).then_inc(x_in, 16)
            sp.dma_start(CS[:], a["rotary"].rearrange("c (t p) r -> p c t r", p=P)).then_inc(cs_in, 16)

            def ada_loads(h, first):
                for t in range(NT):
                    for j in range(4):
                        u = 4 * t + j
                        if not first or u >= 2:
                            sp.wait_ge(ada2_lo, 40 * h + 2 * u - 2)
                        layer = ADA_TILES[t][0]
                        src = ada_w[layer, :, 2 * j:2 * j + 2, bass.ds(ada2_chunk(h, t) * HALF, HALF)]
                        sp.dma_start(ADA_RAW[:, u % 2].rearrange("p (k n) -> p k n", k=2), src).then_inc(ada2_in[u % 2], 16)

            def ret_loads(h, first):
                None if first else sp.wait_ge(qk_mm, 4 * h)
                for w in range(2):
                    sp.dma_start(WQK[:, w], ret_in[:, :, bass.ds(w * D + h * DK, DK)]).then_inc(w_in[0], 16)
                None if first else sp.wait_ge(v_mm, NT * h)
                sp.dma_start(W8[:, 1], ret_in[:, :, bass.ds(2 * D + h * DV, DV)]).then_inc(w_in[1], 16)
                sp.wait_ge(ada_mm, 4) if first else sp.wait_ge(y_mm, NT * h)
                for e, st in enumerate(("state_ret_fwd", "state_ret_bwd")):
                    sp.dma_start(S0[:, e], a[st].rearrange("a b h (m p) e -> (a b h) p m e", p=P)[bass.ds(h, 1)][0]).then_inc(s0_in, 16)
                sp.wait_ge(ada_mm, 1) if first else sp.wait_ge(g_mm, NT * h)
                sp.dma_start(W8[:, 2], ret_in[:, :, bass.ds(2 * D + HEADS * DV + h * DV, DV)]).then_inc(w_in[2], 16)
                sp.wait_ge(ada_mm, 2) if first else sp.wait_ge(out_mm, 2 * NT * h)
                sp.dma_start(W4[:, 3], ret_out[bass.ds(h, 1)][0]).then_inc(w_in[3], 16)

            ret_loads(0, True)
            sp.wait_ge(nt_xn, NT)
            ada_loads(0, True)
            with sp.Fori(1, HEADS) as h:
                ret_loads(h, False)
                ada_loads(h, False)
            sp.wait_ge(ada2_used, 40 * HEADS)
            sp.dma_start(X[:, 0:3, :], a["x_sample"][0, 0:3 * P, :].rearrange("(t p) d -> p t d", p=P)).then_inc(x_back, 16)
            sp.wait_ge(yt_mm, NT * HEADS)
            sp.dma_start(X[:, 3, :], a["x_sample"][0, 3 * P:4 * P, :]).then_inc(x_in, 16)
            sp.dma_start(X[:, NLAT, :], a["x_prompt"][0]).then_inc(x_in, 16)

            def mix_load(layer, base, place, i, unit, fresh):
                e, w, q = unit
                if not fresh:
                    sp.wait_ge(MS_["lo"], 2 * (layer * UNITS + base + i - RAWS + 1))
                src = a[("moe_w_gate", "moe_w_up", "moe_w_down")[w]][layer].rearrange("e (q k p) n -> e q p k n", p=P, k=2)
                slot = (place + i) % RAWS
                sp.dma_start(RAW_W[:, slot].rearrange("p (k n) -> p k n", k=2), src[bass.ds(e, 1)][0, q]).then_inc(raw_in[slot], 16)

            def mix_turn(layer, p, first):
                base, place = first_unit(p, first)
                for i, unit in enumerate(turn_units(p, first)):
                    mix_load(layer, base, place, i, unit, first and i < RAWS)

            def mix_all(layer):
                sp.wait_ge(*((MS_["lg_mm"], layer) if layer else (dec_ready, 5 * HEADS)))
                sp.dma_start(WR, a["moe_w_router"][layer].rearrange("(k p) e -> p k e", p=P)).then_inc(wr_in, 16)
                sp.wait_ge(*((MA["mo_mm"], 2 * NT) if layer else (v_mm, NT * HEADS)))
                mix_turn(layer, 0, True)
                with sp.Fori(1, PAIRS) as p:
                    mix_turn(layer, p, False)
                for q in range(4):
                    mix_load(layer, 24 * PAIRS - 4, 20, q, (NE - 1, 2, q), False)

            def mla_loads():
                sp.wait_ge(MS_["lo"], 2 * UNITS)
                wi = a["mla_w_in"][0].rearrange("(g k p) n -> g p k n", p=P, k=4)
                for g in range(2):
                    sp.dma_start(WIN2[g], wi[g]).then_inc(w_in[g], 16)
                sp.wait_ge(MS_["used"], 2 * UNITS)
                wq = a["mla_w_q_b"][0].rearrange("(k p) (g n) -> g p k n", p=P, g=2)
                for g in range(2):
                    sp.dma_start(W[:, 2 + g, 0:2304].rearrange("p (k n) -> p k n", k=3), wq[g]).then_inc(w_in[2 + g], 16)
                sp.wait_ge(MS_["c_mm"], 10 * PAIRS)
                sp.dma_start(CKC, a["cache_mla_ckv"][0, 0]).then_inc(MA["ctx_in"], 16)
                for j in range(2):
                    sp.dma_start(KRD[:, 0, j * ROPE:(j + 1) * ROPE], a["cache_mla_krope"][0, 0]).then_inc(MA["ctx_in"], 16)
                sp.dma_start(KVG, a["mla_kv_norm"].to_broadcast([P, KVL])).then_inc(MA["ctx_in"], 16)
                wo = a["mla_w_out"][0].rearrange("(g k p) n -> g p k n", p=P, k=4)
                sp.wait_ge(MA["lat_mm"], NT)
                sp.dma_start(W[:, 0, :].rearrange("p (k n) -> p k n", k=2),
                             a["mla_w_kv_b"][0].rearrange("(k p) n -> p k n", p=P)).then_inc(w_in[0], 16)
                sp.dma_start(W4[:, 1], wo[0]).then_inc(w_in[1], 16)
                sp.wait_ge(MA["lat_ev"], NT)
                sp.dma_start(o["new_krope"][0, 0], LATN[:, NLAT, QL + KVL:WIN]).then_inc(MA["new_out"], 16)
                sp.wait_ge(MA["cko"], 1)
                sp.dma_start(o["new_ckv"][0, 0], CKO).then_inc(MA["new_out"], 16)
                sp.wait_ge(MA["kn_mm"], MH)
                sp.dma_start(W4[:, 2], wo[1]).then_inc(w_in[2], 16)

            if STAGE >= 2:
                mix_all(0)
            if STAGE >= 3:
                mla_loads()
                mix_all(1)
            n_x = {1: 1, 2: 2, 3: 4}[STAGE]
            for t in range(NT):
                sp.wait_ge(x_ready, NT * (n_x - 1) + t + 1)
                dst = o["y_sample"][0, t * P:(t + 1) * P, :] if t < NLAT else o["y_prompt"][0]
                sp.dma_start(dst, X[:, t, :]).then_inc(stored, 16)
            sp.wait_ge(stored, 16 * NT)

        @block.gpsimd
        def _(pool):
            chain = Chain(pool, pool_chain)
            chain.link(nc.gpsimd.memset(IDENT[:], 0.0))
            nc.gpsimd.affine_select(out=IDENT[:], in_=IDENT[:], compare_op=ALU.not_equal, fill=1.0,
                                    base=0, pattern=[[-1, P]], channel_multiplier=1).then_inc(const_ready, 1)
            nc.gpsimd.memset(ONES[:], 1.0).then_inc(const_ready, 1)
            nc.gpsimd.memset(EPSC, EPS).then_inc(const_ready, 1)
            nc.gpsimd.memset(NHALF, -0.5).then_inc(const_ready, 1)
            kw = dict(allow_small_or_imprecise_dtypes=True)
            nc.gpsimd.iota(SLOTNO[:], [[1, CAP]], base=1, channel_multiplier=0, **kw).then_inc(const_ready, 1)
            nc.gpsimd.iota(STEP1[:], [[1, LAT]], base=1, channel_multiplier=0, **kw).then_inc(const_ready, 1)
            nc.gpsimd.iota(TPOS[:, 0:1], [[1, 1]], base=P - 1, channel_multiplier=-1, **kw).then_inc(const_ready, 1)
            nc.gpsimd.iota(TPOS[:, 1:2], [[1, 1]], base=0, channel_multiplier=1, **kw).then_inc(const_ready, 1)
            pool.wait_ge(ada_mm, ADA_FIRST)
            nc.gpsimd.iota(DIFF, [[1, 896]], base=-384, channel_multiplier=-1, **kw).then_inc(const_ready, 1)

            def rstd(t, source, needs, ss, ms, out, ready):
                pool.wait_ge(source, needs)
                t = slice(t, t + 1)
                chain.link(nc.gpsimd.tensor_scalar(ms[:, t], ss[:, t], 1.0 / D, EPS, ALU.mult, ALU.add))
                nc.gpsimd.tensor_tensor(out[:, t], ms[:, t], NHALF[:, t], ALU.pow).then_inc(ready, 1)

            def update_rstd(n, t):
                if 0 <= t < NT:
                    rstd(t, ru_ss, NT * n + t + 1, SSU, MSU, RSTDU, ru_rstd)

            def norm_rstd(n, t):
                if 0 <= t < NT:
                    rstd(t, nt_ss, NT * n + t + 1, SSN, MSN, RSTDN, nt_rstd)

            for t in range(NT):
                norm_rstd(0, t)

            def ret_head(h, last):
                for t in range(NT):
                    pool.wait_ge(var_ready, NT * h + t + 1)
                    chain.link(nc.gpsimd.tensor_tensor(RV[:, t:t + 1], MV[:, 2 * t + 1:2 * t + 2], EPSC, ALU.add))
                    nc.gpsimd.tensor_tensor(RSY[:, t:t + 1], RV[:, t:t + 1], NHALF[:, 0:1], ALU.pow).then_inc(rsy_ready, 1)
                    if last:
                        update_rstd(0, t - 2)
                        norm_rstd(1, t - 3)

            ret_head(0, False)
            with pool.Fori(1, HEADS - 1) as h:
                chain.enter(h, 1, NT)
                ret_head(h, False)
            chain.leave(HEADS - 2)
            ret_head(HEADS - 1, True)
            for t in range(NT, NT + 3):
                update_rstd(0, t - 2)
                norm_rstd(1, t - 3)

            def mix_pool(layer):
                pool.wait_ge(MS_["lg_mm"], layer + 1)
                nc.gpsimd.memset(YB2, 0.0)
                nc.gpsimd.memset(YE_HI[:, 1].bitcast(F32), 0.0)
                nc.gpsimd.memset(YE_LO[:, 1].bitcast(F32), 0.0).then_inc(MS_["zero"], 1)
                for t in range(NT + 2):
                    update_rstd(2 * layer + 1, t)
                    if not layer:
                        norm_rstd(2, t - 2)

            if STAGE >= 2:
                mix_pool(0)
            if STAGE >= 3:
                pool.wait_ge(MA["lat_ss"], 2 * NT)
                nc.gpsimd.tensor_scalar(LMS[:, 0:NT], LSS[:, 0:NT], 1.0 / QL, EPS, ALU.mult, ALU.add)
                chain.link(nc.gpsimd.tensor_scalar(LMS[:, NT:2 * NT], LSS[:, NT:2 * NT], 1.0 / KVL, EPS, ALU.mult, ALU.add))
                for j in range(2):
                    nc.gpsimd.tensor_tensor(LRS[:, j * NT:(j + 1) * NT], LMS[:, j * NT:(j + 1) * NT], NHALF, ALU.pow).then_inc(MA["lat_rstd"], 1)
                for t in range(NT + 1):
                    update_rstd(2, t)
                    norm_rstd(3, t - 1)
                mix_pool(1)
        @block.scalar
        def _(act):
            act.wait_ge(lu_ready, 1)
            nc.scalar.activation(LV, LV, ACT.Exp).then_inc(lu_ready, 1)
            act.wait_ge(cols_tr, 1)
            nc.scalar.activation(NCOL[:, COND:QN], ps[:, 4, COND:QN], ACT.Silu).then_inc(cond_ready, 1)
            act.wait_ge(cols_tr, 3)
            act_copy(BCOL[:, 0, :], ps[:, 5, 0:48]).then_inc(cols_ev, 1)
            act_copy(BCOL[:, 1, :], ps[:, 6, 0:48]).then_inc(cols_ev, 1)
            act_copy(NCOL[:, 0:COND], ps[:, 4, 0:COND]).then_inc(cols_ev, 1)
            act_copy(NCOL[:, QN:COLS], ps[:, 4, QN:COLS]).then_inc(cols_ev, 1)
            act.wait_ge(cond_ready, 1)
            act_copy(COND_HL[:, :, 0:2], NCOL[:, COND:QN].rearrange("p (c k) -> p k c", c=2)).then_inc(cond_hi, 1)
            for n in range(ADA_FIRST):
                act.wait_ge(ada_mm, n + 1)
                if n >= 2:
                    act.wait_ge(ada_tr, n - 1)
                act_copy(AROW[0:2, n % 2, :], ps[0:2, n % 2, :]).then_inc(ada_ev, 1)

            def norm_squares(n, t, x_sem, x_needs):
                if 0 <= t < NT:
                    act.wait_ge(x_sem, x_needs)
                    nc.scalar.activation(B1[:, t, :], X[:, t, :], ACT.Square, accum_out=SSN[:, t:t + 1]).then_inc(nt_ss, 1)

            def norm_act(n, layer, sub):
                for t in range(NT):
                    act.wait_ge(nt_tr, 10 * n + 2 * t + 2)
                    c = t // NLAT
                    for k in range(4, 8):
                        last = nc.scalar.activation(HT[:, k, t * P:(t + 1) * P], ps[:, 5 + 2 * (t % 2), (k - 4) * P:(k - 3) * P],
                                                    ACT.Identity, scale=scale_col(layer, sub, k, c), bias=shift_col(layer, sub, k, c))
                    last.then_inc(nt_eva, 1)

            def gates_act(n):
                for j in range(4):
                    act.wait_ge(gate_mm, 4 * n + j + 1)
                    act_copy(GATE[:, j // 2, (j % 2) * HALF:(j % 2 + 1) * HALF], ps[:, j, :]).then_inc(gate_ev, 1)

            def update_squares(n, t, Y, squares, ready, needs):
                if 0 <= t < NT:
                    act.wait_ge(ready, needs)
                    if t:
                        act.wait_ge(ru_ss, NT * n + t)
                    nc.scalar.activation(squares, Y[:, t, :], ACT.Square, accum_out=SSU[:, t:t + 1]).then_inc(ru_ss, 1)

            for t in range(NT):
                norm_squares(0, t, x_in, 32)
            act.wait_ge(ada_ready, 1)
            norm_act(0, 0, 0)

            def ada_hi(h, first, i):
                act.wait_ge(ada2_in[i // 2 % 2], 160 * h + 16 * (i // 4 + 1))
                if not first or i >= 2:
                    act.wait_ge(ada2_used, 40 * h + i - 1)
                act_copy(ADA_HI[:, i % 2], ADA_RAW[:, i // 2 % 2, i % 2 * HALF:(i % 2 + 1) * HALF]).then_inc(ada2_hi, 1)

            def value_tile(h, first, t):
                act.wait_ge(ada2_used, 40 * h + KD * (t + 1))
                if not first or t >= 2:
                    act.wait_ge(ada2_tr, NT * h + t - 1 if t >= 2 else NT * h)
                act_copy(ROWS4[0:4, t % 2, :], ps[0:4, 6 + t % 2, :]).then_inc(ada2_ev, 1)
                act.wait_ge(v_mm, NT * h + t + 1)
                act_copy(V[:, t, :], ps[:, 4 + t % 2, :]).then_inc(v_ev, 1)

            def ret_head(h, first, last):
                act.wait_ge(te_ready, h + 1)
                nc.scalar.activation(DEC, DEC, ACT.Exp).then_inc(dec_ready, 1)
                nc.scalar.activation(CROSS[:, 0, :], STEP1[:], ACT.Exp, scale=LG[:, bass.ds(h, 1)]).then_inc(dec_ready, 1)
                nc.scalar.activation(CROSS[:, 1, :], STEP1[:], ACT.Exp, scale=NLGB[:, bass.ds(h, 1)], bias=LGB513[:, bass.ds(h, 1)]).then_inc(dec_ready, 1)
                nc.scalar.activation(KDEC[:, 0:1], TPOS[:, 0:1], ACT.Exp, scale=LG[:, bass.ds(h, 1)]).then_inc(dec_ready, 1)
                nc.scalar.activation(KDEC[:, 1:2], TPOS[:, 1:2], ACT.Exp, scale=LG[:, bass.ds(h + 4, 1)]).then_inc(dec_ready, 1)
                for u in range(4):
                    act.wait_ge(qk_mm, 4 * h + u + 1)
                    dst, scale = (QT, 1.0) if u < 2 else (KT, DK ** -0.5)
                    b = 2 * (u % 2)
                    act_copy(dst[:, u % 2, 0:LAT], ps[:, b, :], scale)
                    act_copy(dst[:, u % 2, LAT:TOK], ps[:, b + 1, 0:P], scale).then_inc(qk_ev, 1)
                    if u == 1:
                        ada_hi(h, first, 0)
                        ada_hi(h, first, 1)
                for i in range(2, KD * NT):
                    ada_hi(h, first, i)
                    if i % KD == 1:
                        value_tile(h, first, i // KD - 1)
                value_tile(h, first, NT - 1)
                for t in range(NT + 1):
                    if t >= 1:
                        u = t - 1
                        act.wait_ge(yt_mm, NT * h + u + 1)
                        if u >= 2 or not first:
                            act.wait_ge(out_mm, 2 * NT * h + 2 * (u - 1) if u >= 2 else 2 * NT * h)
                        act_copy(YT[:, u % 2], ps[:, 4 + u % 2, :].rearrange("p (c t) -> p c t", c=4)).then_inc(yt_ev, 1)
                    if t < NT:
                        act.wait_ge(g_mm, NT * h + t + 1)
                        if t >= 2 or not first:
                            act.wait_ge(yn_done, NT * h + t - 1 if t >= 2 else NT * h)
                        if t < 2 and not first:
                            act.wait_ge(st_out[2 + t], 16 * h)
                        nc.scalar.activation(SILG[:, t % 2, :], ps[:, 2 + t % 2, :], ACT.Silu).then_inc(silg, 1)
                    if last:
                        finish(t)
                for j in range(4):
                    act.wait_ge(st_mm, 4 * h + j + 1)
                    if not first and j < 2:
                        act.wait_ge(st_out[j], 16 * h)
                    act_copy(STATES[j], ps[:, j, :]).then_inc(st_ev, 1)
                    act.wait_ge(st_ev, 4 * h + j + 1)
                    dst = o[("state_fwd", "state_bwd")[j // 2]].rearrange("a b h (m p) e -> (a b h) m p e", p=P)
                    act.dma_start(dst[bass.ds(h, 1)][0, j % 2], STATES[j]).then_inc(st_out[j], 16)

            def finish(t):
                update_squares(0, t - 2, B1, CROSS, out_acc, 2 * NT * (HEADS - 1) + 2 * (t - 1))
                norm_squares(1, t - 3, x_ready, t - 2)

            ret_head(0, True, False)
            gates_act(0)
            with act.Fori(1, HEADS - 1) as h:
                ret_head(h, False, False)
            ret_head(HEADS - 1, False, True)
            finish(NT + 1)
            finish(NT + 2)
            for j in range(4):
                act.wait_ge(st_out[j], 16 * HEADS)

            def mix_act(layer):
                b = {n: layer * v for n, v in per_layer.items()}
                norm_act(2 * layer + 1, layer, 1)
                act.wait_ge(MS_["lg_mm"], b["lg_mm"] + 1)
                act_copy(SEL[0:NE], ps[0:NE, 0:2, :].rearrange("p a n -> p (a n)")[:, 0:TOK]).then_inc(MS_["lt_ev"], 1)
                act.wait_ge(MS_["lgs"], b["lgs"] + 1)
                nc.scalar.activation(LGS, LGS, ACT.Exp).then_inc(MS_["ex"], 1)
                def split_hi(base, place, lo, hi):
                    for i in range(lo, hi):
                        unit = (place + i) // 2
                        act.wait_ge(raw_in[unit % RAWS], 16 * (UNITS // RAWS * layer + unit // RAWS + 1) + 2 * (base - place))
                        if place + i >= SPLITS:
                            act.wait_ge(MS_["used"], b["used"] + base + i - SPLITS + 1)
                        at = i % 2 * PART
                        act_copy(W_HI[:, (place + i) % SPLITS], RAW_W[:, unit % RAWS, at:at + PART]).then_inc(MS_["hi"], 1)

                def sil(e, done):
                    act.wait_ge(MS_["used"], b["used"] + done)
                    nc.scalar.activation(HID[0:ROWS, :].rearrange("p (a n) -> p a n", a=2), ps[0:ROWS, 0:2, :], ACT.Silu).then_inc(MS_["sil"], 1)

                def hidden(e, done):
                    act.wait_ge(MS_["used"], b["used"] + done)
                    for half in range(2):
                        act.wait_ge(MS_["t_mm"], b["t_mm"] + 2 * e + half + 1)
                        act_copy(HTE_HI[:, 4 * half:4 * half + 4, :], ps[:, 6 + half, 0:4 * ROWS].rearrange("p (c r) -> p c r", c=4)).then_inc(MS_["t_ev"], 1)

                def expert_out(odd, done):
                    act.wait_ge(MS_["used"], b["used"] + done)
                    at = 64 * odd
                    act_copy(YE_HI[at:at + CAP, 0, :].rearrange("p (a n) -> p a n", a=2), ps[0:CAP, 4:6, :])
                    act_copy(YE_HI[at:at + CAPP, 1, :].rearrange("p (a n) -> p a n", a=2), ps[CAP:ROWS, 4:6, :]).then_inc(MS_["y_ev"], 1)

                def split_tokens(pair, odd, done):
                    act.wait_ge(MS_["xt_ev"], b["xt_ev"] + 3 * (pair + 1))
                    if done is not None:
                        act.wait_ge(MS_["used"], b["used"] + done)
                    act_copy(XET_HI[:, odd], XET[:, odd]).then_inc(MS_["xh"], 1)

                def combine_rows(pair):
                    for half in range(2):
                        act.wait_ge(MS_["ct_mm"], b["ct_mm"] + 2 * pair + half + 1)
                        if half == 0:
                            act_copy(CT_HI[:, 0:4, :], ps[:, 6, :].rearrange("p (t n) -> p t n", t=4)).then_inc(MS_["ct_ev"], 1)
                        else:
                            act_copy(CT_HI[:, 4, :], ps[:, 7, 0:P]).then_inc(MS_["ct_ev"], 1)

                split_hi(0, 0, 0, AHEAD)
                split_tokens(0, 0, None)
                split_tokens(0, 1, None)

                def turn(p, first, last):
                    base, place = first_part(p, first)
                    up_a, down_b, up_b, down_a = turn_parts(first)
                    at = AHEAD

                    def split_until(done):
                        nonlocal at
                        split_hi(base, place, at, done + AHEAD)
                        at = done + AHEAD

                    split_until(up_a)
                    sil(2 * p, base + up_a)
                    if not last:
                        split_until(up_a + 2)
                        split_tokens(p + 1, 0, base + up_a)
                    split_until(down_b + 4 * first)
                    hidden(2 * p, base + down_b)
                    if not first:
                        expert_out(1, base + down_b)
                        split_until(down_b + 5)
                        combine_rows(p - 1)
                    split_until(up_b)
                    sil(2 * p + 1, base + up_b)
                    if not last:
                        split_until(up_b + 2)
                        split_tokens(p + 1, 1, base + up_b)
                    split_until(down_a)
                    hidden(2 * p + 1, base + down_a)
                    expert_out(0, base + down_a)

                turn(0, True, False)
                with act.Fori(1, PAIRS - 1) as p:
                    turn(p, False, False)
                turn(PAIRS - 1, False, True)
                split_hi(*first_part(PAIRS, False), AHEAD, 2 * DOWN)
                combine_rows(PAIRS - 1)
                gates_act(2 * layer + 1)
                expert_out(1, 2 * UNITS)
                n = 2 * layer + 1
                for t in range(NT + 2):
                    update_squares(n, t, YB2, B1[:, t % NT, :], MS_["c_ev"], b["c_ev"] + 10 * (PAIRS - 1) + 2 * (t + 1))
                    if not layer:
                        norm_squares(n + 1, t - 2, x_ready, NT * n + t - 1)
                act.wait_ge(x_ready, NT * (n + 1))

            def mla_act():
                norm_act(2, 1, 0)
                for t in range(NT):
                    act.wait_ge(MA["lat_mm"], t + 1)
                    b = 2 * (t % 2)
                    act_copy(LATN[:, t, :], ps[:, b:b + 2, :].rearrange("p a n -> p (a n)")[:, 0:WIN]).then_inc(MA["lat_ev"], 1)
                    act.wait_ge(MA["lat_ev"], t + 1)
                    nc.scalar.activation(B1[:, t, 0:QL], LATN[:, t, 0:QL], ACT.Square, accum_out=LSS[:, t:t + 1]).then_inc(MA["lat_ss"], 1)
                    nc.scalar.activation(B1[:, t, QL:QL + KVL], LATN[:, t, QL:QL + KVL], ACT.Square, accum_out=LSS[:, NT + t:NT + t + 1]).then_inc(MA["lat_ss"], 1)
                gates_act(2)
                for kt in range(NK):
                    act.wait_ge(MA["kv_tr"], kt + 1)
                    for c in range(2):
                        dst, src = KVT[:, c, kt * P:(kt + 1) * P], ps[:, 6 + kt % 2, c * P:(c + 1) * P]
                        if kt == 0:
                            act_copy(dst, src)
                        else:
                            nc.scalar.activation(dst, src, ACT.Identity, scale=NCOL[:, KVN + c:KVN + c + 1])
                    act_copy(KRT[:, kt * P:(kt + 1) * P], ps[:, 6 + kt % 2, 2 * P:3 * P]).then_inc(MA["kv_ev"], 1)
                act.wait_ge(MA["new_out"], 32)
                for t in range(NT):
                    act.wait_ge(MA["qr_mm"], t + 1)
                    act_copy(QR[:, t, :], ps[:, t % 4, :]).then_inc(MA["qr_ev"], 1)
                for kt in range(NK):
                    for half in range(2):
                        act.wait_ge(MA["vv_mm"], 2 * kt + half + 1)
                        dst = B1[:, kt, half * HALF:(half + 1) * HALF] if kt < NT else VP[:, half * HALF:(half + 1) * HALF]
                        act_copy(dst, ps[:, 6 + half, :]).then_inc(MA["vv_ev"], 1)
                for t in range(NT):
                    act.wait_ge(MA["qrt_tr"], t + 1)
                    act_copy(QRT[:, :, t * P:(t + 1) * P], ps[:, 4 + t % 2, :].rearrange("p (c t) -> p c t", c=4)).then_inc(MA["qrt_ev"], 1)

                def exps(h, t):
                    n = NT * h + t
                    act.wait_ge(MA["nm"], n + 1)
                    if n >= 2:
                        act.wait_ge(MA["pt_tr"], n - 1)
                    b = (4, 6, 4, 6, 4)[t]
                    width = LAT + P if t < NLAT else P
                    src = ps[:, b:b + 2, :].rearrange("p a n -> p (a n)")[:, 0:width]
                    nc.scalar.activation(PR[:, n % 2, 0:width], src, ACT.Exp, scale=ATT_SCALE, bias=RNM[:, n % 2:n % 2 + 1],
                                         accum_out=RSM[:, n % 2:n % 2 + 1]).then_inc(MA["e_done"], 1)

                def projected(h, n):
                    act.wait_ge(MA["kn_mm"], 2 * h + n + 1)
                    dst = (KNT, QNT)[n][:, h % 2, :]
                    act_copy(dst, ps[:, 2:4, :].rearrange("p a n -> p (a n)")[:, 0:(NK * P, TOK)[n]]).then_inc(MA["kn_ev"], 1)

                projected(0, 0)
                projected(0, 1)
                for h in range(MH):
                    exps(h, 0)
                    for t in range(NT):
                        if t + 1 < NT:
                            exps(h, t + 1)
                        if t in (1, 2) and h + 1 < MH:
                            projected(h + 1, t - 1)
                        act.wait_ge(MA["pt_tr"], NT * h + t + 1)
                        if t < NLAT:
                            src = ps[:, 0:2, :].rearrange("p a n -> p (a n)")[:, 0:LAT + P].rearrange("p (k q) -> p k q", q=P)
                            act_copy(PT[:, :, t * P:(t + 1) * P], src).then_inc(MA["pt_ev"], 1)
                        else:
                            act_copy(PTP, ps[:, 0, 0:P]).then_inc(MA["pt_ev"], 1)
                squares = KNT.rearrange("p b n -> p (b n)")[:, 0:D]
                for t in range(NT + 1):
                    if t < NT:
                        for half in range(2):
                            act.wait_ge(MA["mo_mm"], 2 * t + half + 1)
                            act_copy(B1[:, t, half * HALF:(half + 1) * HALF], ps[:, 4 + 2 * (t % 2) + half, :]).then_inc(MA["mo_ev"], 1)
                    update_squares(2, t, B1, squares, MA["mo_ev"], 2 * (t + 1))
                    norm_squares(3, t - 1, x_ready, 2 * NT + t)

            if STAGE >= 2:
                mix_act(0)
            if STAGE >= 3:
                mla_act()
                mix_act(1)

        @block.vector
        def _(dve):
            chain = Chain(dve, dve_chain)
            V_ = nc.vector
            dve.wait_ge(dec_in, 32)
            chain.link(V_.tensor_scalar(LV, LU, -1.0, None, ALU.mult))
            chain.link(V_.tensor_tensor(LV, LV, LU, ALU.min))
            chain.link(V_.tensor_scalar(LU, LU, 0.0, None, ALU.min))
            V_.memset(LW, 0.0).then_inc(lu_ready, 1)
            dve.wait_ge(lu_ready, 2)
            chain.link(V_.tensor_scalar(LW, LV, 2.0, None, ALU.add))
            chain.link(V_.reciprocal(LW, LW))
            chain.link(V_.tensor_tensor(LV, LV, LW, ALU.mult))
            chain.link(V_.tensor_tensor(LW, LV, LV, ALU.mult))
            chain.link(V_.tensor_scalar(LG, LW, 1.0 / 17, 1.0 / 15, ALU.mult, ALU.add))
            for n in (13, 11, 9, 7, 5, 3, 1):
                chain.link(V_.tensor_tensor(LG, LG, LW, ALU.mult))
                chain.link(V_.tensor_scalar(LG, LG, 1.0 / n, None, ALU.add))
            chain.link(V_.tensor_tensor(LG, LG, LV, ALU.mult))
            chain.link(V_.scalar_tensor_tensor(LG, LG, -2.0, LU, ALU.mult, ALU.add))
            chain.link(V_.tensor_scalar(NLGB, LG[:, 4:8], -1.0, None, ALU.mult))
            chain.link(V_.tensor_scalar(LGB513, LG[:, 4:8], float(LAT + 1), None, ALU.mult))
            dve.wait_ge(cond_hi, 1)
            V_.tensor_tensor(COND_HL[:, :, 2:4], NCOL[:, COND:QN].rearrange("p (c k) -> p k c", c=2),
                             COND_HL[:, :, 0:2].bitcast(F32), ALU.subtract).then_inc(cond_lo, 1)
            dve.wait_ge(cols_ev, 4)
            for n in range(ADA_FIRST):
                dve.wait_ge(ada_tr, n + 1)
                cols = ADA[:, 0].rearrange("p j k c -> p (j k) c")[:, 4 * n:4 * n + 4, :]
                bias = BCOL[:, 0, 4 * n:4 * n + 4].unsqueeze(2).to_broadcast([P, 4, 2])
                V_.tensor_tensor(cols, ps[:, 2 + n % 2, 0:8].rearrange("p (k c) -> p k c", k=4), bias, ALU.add).then_inc(ada_col, 1)

            def scale_gain(layer, sub):
                sc = ADA[:, layer, 3 * sub + 1]
                return V_.scalar_tensor_tensor(sc, sc, 1.0, norm_col("pre", layer, sub).unsqueeze(2).to_broadcast([P, KD, 2]), ALU.add, ALU.mult)

            def gate_gain(layer, sub):
                g = ADA[:, layer, 3 * sub + 2]
                return V_.tensor_tensor(g, g, norm_col("post", layer, sub).unsqueeze(2).to_broadcast([P, KD, 2]), ALU.mult)

            dve.wait_ge(ada_col, ADA_FIRST)
            scale_gain(0, 0).then_inc(ada_ready, 1)
            dve.wait_ge(ada_ready, 1)

            def ada_lo(h, i):
                dve.wait_ge(ada2_hi, 40 * h + i + 1)
                V_.tensor_tensor(ADA_LO[:, i % 2], ADA_RAW[:, i // 2 % 2, i % 2 * HALF:(i % 2 + 1) * HALF],
                                 ADA_HI[:, i % 2].bitcast(F32), ALU.subtract).then_inc(ada2_lo, 1)

            def ada_cols(h, t):
                dve.wait_ge(ada2_tr, NT * h + t + 1)
                layer = ADA_TILES[t][0]
                at = bass.ds(4 * ada2_chunk(h, t), 4)
                cols = ADA[:, layer].rearrange("p j k c -> p (j k) c")[:, at, :]
                parts = ps[:, 2 + t % 2, 0:16].rearrange("p (q c) -> p q c", q=4)
                chain.link(V_.tensor_tensor(cols, parts[:, :, 0:2], BCOL[:, layer, at].unsqueeze(2).to_broadcast([P, 4, 2]), ALU.add))
                V_.tensor_tensor(cols, cols, parts[:, :, 2:4], ALU.add).then_inc(ada2_col, 1)

            def normalise(n, t):
                if 0 <= t < NT:
                    dve.wait_ge(nt_rstd, NT * n + t + 1)
                    V_.tensor_scalar(B1[:, t, :], X[:, t, :], RSTDN[:, t:t + 1], None, ALU.mult).then_inc(nt_xn, 1)

            def norm_dve(n, layer, sub):
                for t in range(NT):
                    dve.wait_ge(nt_tr, 10 * n + 2 * t + 1)
                    c = t // NLAT
                    for k in range(4):
                        last = V_.tensor_scalar(HT[:, k, t * P:(t + 1) * P], ps[:, 4 + 2 * (t % 2), k * P:(k + 1) * P],
                                                scale_col(layer, sub, k, c), shift_col(layer, sub, k, c), ALU.mult, ALU.add)
                    last.then_inc(nt_evd, 1)

            def gates_dve(n, layer, sub, diag):
                for j in range(4):
                    if j >= 2:
                        dve.wait_ge(gate_mm, 4 * n + j - 1)
                    for q in range(4):
                        k = 4 * (j % 2) + q
                        last = V_.tensor_scalar(diag[:, j % 2, q * P:(q + 1) * P], IDENT[:], ADA[:, layer, 3 * sub + 2, k, j // 2:j // 2 + 1], None, ALU.mult)
                    last.then_inc(gate_diag, 1)

            def update(n, t, Y):
                if 0 <= t < NT:
                    dve.wait_ge(ru_rstd, NT * n + t + 1)
                    if t == 0:
                        dve.wait_ge(gate_ev, 4 * (n + 1))
                    chain.link(V_.scalar_tensor_tensor(Y[:, t, :], Y[:, t, :], RSTDU[:, t:t + 1], GATE[:, t // NLAT, :], ALU.mult, ALU.mult))
                    V_.tensor_tensor(X[:, t, :], X[:, t, :], Y[:, t, :], ALU.add).then_inc(x_ready, 1)

            dve.wait_ge(const_ready, 9)
            for t in range(NT):
                normalise(0, t)
            norm_dve(0, 0, 0)

            def qx(h, t):
                for e in range(2):
                    last = V_.tensor_tensor(QX[:, t % 2, e], QT[:, :, t * P:(t + 1) * P],
                                            CROSS[:, e, t * P:(t + 1) * P].unsqueeze(1).to_broadcast([P, 2, P]), ALU.mult)
                last.then_inc(qx_ready, 1)

            def ret_head(h, first, final):
                if not first:
                    dve.wait_ge(y_mm, NT * h)
                chain.link(V_.tensor_scalar(DEC, DIFF, 0.0, LG[:, bass.ds(h, 1)], ALU.max, ALU.mult))
                chain.link(V_.tensor_scalar(DTMP, DIFF, 0.0, NLGB[:, bass.ds(h, 1)], ALU.min, ALU.mult))
                V_.tensor_tensor(DEC, DEC, DTMP, ALU.add).then_inc(te_ready, 1)
                for i in range(KD * NT):
                    ada_lo(h, i)
                    if i % KD == 6 and i > KD:
                        ada_cols(h, i // KD - 1)
                ada_cols(h, NT - 1)
                if final:
                    dve.wait_ge(ada2_col, NT * HEADS)
                    for layer, sub in ((0, 1), (1, 0), (1, 1)):
                        scale_gain(layer, sub)
                        done = gate_gain(layer, sub)
                    done.then_inc(ada_ready, 1)
                dve.wait_ge(dec_ready, 5 * (h + 1))
                dve.wait_ge(qk_ev, 4 * (h + 1))
                for t in range(NLAT):
                    dve.wait_ge(sc_mm, NT * h + t + 1)
                    lo = 384 - P * t
                    V_.tensor_tensor(SC[:, t, :], ps[:, t, :], DEC[:, lo:lo + LAT], ALU.mult).then_inc(sc_ev, 1)
                dve.wait_ge(sc_mm, NT * (h + 1))
                V_.tensor_tensor(SCP, ps[:, 6, 0:P], DEC[:, 384:384 + P], ALU.mult).then_inc(sc_ev, 1)
                qx(h, 0)
                qx(h, 1)
                dve.wait_ge(kp_mm, h + 1)
                for e in range(2):
                    last = V_.tensor_scalar(KP[:, e, :], ps[:, 7, 0:DK], KDEC[:, e:e + 1], None, ALU.mult)
                last.then_inc(kp_ev, 1)
                for t in range(NT + 1):
                    if t < NT:
                        dve.wait_ge(y_mm, NT * h + t + 1)
                        chain.link(V_.bn_stats(BST, ps[:, t % 2, :]))
                        V_.memset(IDLE, 0.0)
                        V_.bn_aggr(MV[:, 2 * t:2 * t + 2], BST).then_inc(var_ready, 1)
                        dve.wait_ge(var_ready, NT * h + t + 1)
                        dve.wait_ge(silg, NT * h + t + 1)
                        if t >= 2 or not first:
                            dve.wait_ge(yt_mm, NT * h + t - 1 if t >= 2 else NT * h)
                        V_.scalar_tensor_tensor(YN[:, t % 2, :], ps[:, t % 2, :], MV[:, 2 * t:2 * t + 1], SILG[:, t % 2, :],
                                                ALU.subtract, ALU.mult).then_inc(yn_done, 1)
                        if t + 2 < NLAT:
                            qx(h, t + 2)
                    if t >= 1:
                        u = t - 1
                        dve.wait_ge(rsy_ready, NT * h + u + 1)
                        for half in range(2):
                            dve.wait_ge(out_mm, 2 * NT * h + 2 * u + half + 1)
                            dst = B1[:, u, half * HALF:(half + 1) * HALF]
                            if first:
                                V_.tensor_scalar(dst, ps[:, 6 + half, :], RSY[:, u:u + 1], None, ALU.mult).then_inc(out_acc, 1)
                            else:
                                V_.scalar_tensor_tensor(dst, ps[:, 6 + half, :], RSY[:, u:u + 1], dst, ALU.mult, ALU.add).then_inc(out_acc, 1)
                    if final:
                        finish(t)

            def finish(t):
                if t == 2:
                    dve.wait_ge(x_back, 16)
                if t == 5:
                    dve.wait_ge(x_in, 64)
                update(0, t - 2, B1)
                normalise(1, t - 3)

            ret_head(0, True, False)
            dve.wait_ge(ada2_col, NT)
            gate_gain(0, 0).then_inc(ada_ready, 1)
            dve.wait_ge(ada_ready, 2)
            gates_dve(0, 0, 0, ROWS4)
            with dve.Fori(1, HEADS - 1) as h:
                chain.enter(h, 1, 2 + 2 * NT)
                ret_head(h, False, False)
            chain.leave(HEADS - 2)
            ret_head(HEADS - 1, False, True)
            finish(NT + 1)
            finish(NT + 2)

            def mix_dve(layer):
                b = {n: layer * v for n, v in per_layer.items()}
                n = 2 * layer + 1
                norm_dve(n, layer, 1)
                logits = ps[:, 3, 0:NT * NE].rearrange("p (t e) -> p t e", t=NT)
                dve.wait_ge(MS_["lgt"], b["lgt"] + 1)
                chain.link(V_.tensor_reduce(MX, logits, AX, ALU.max))
                V_.tensor_tensor(LGS, logits, MX.unsqueeze(2).to_broadcast([P, NT, NE]), ALU.subtract).then_inc(MS_["lgs"], 1)
                dve.wait_ge(MS_["ex"], b["ex"] + 1)
                chain.link(V_.tensor_reduce(RC, LGS, AX, ALU.add))
                chain.link(V_.reciprocal(RC, RC))
                V_.tensor_tensor(AFF, LGS, RC.unsqueeze(2).to_broadcast([P, NT, NE]), ALU.mult).then_inc(MS_["aff"], 1)
                dve.wait_ge(MS_["afft"], b["afft"] + 1)
                V_.tensor_copy(WK[0:NE, 0:LAT], ps[0:NE, 1, :])
                chain.link(V_.tensor_copy(WK[0:NE, LAT:TOK], ps[0:NE, 2, 0:P]))
                for lo, hi, cap in ((0, LAT, CAP), (LAT, TOK, CAPP)):
                    for _ in range(cap // 8):
                        chain.link(V_.max(M8[0:NE], WK[0:NE, lo:hi]))
                        chain.link(V_.match_replace(WK[0:NE, lo:hi], M8[0:NE], WK[0:NE, lo:hi], -1.0))
                chain.link(V_.tensor_scalar(SEL[0:NE], WK[0:NE], 0.0, None, ALU.is_lt))
                V_.tensor_tensor_scan(POS[0:NE, 0:LAT], SEL[0:NE, 0:LAT], SEL[0:NE, 0:LAT], 0.0, ALU.add, ALU.max)
                chain.link(V_.tensor_tensor_scan(POS[0:NE, LAT:TOK], SEL[0:NE, LAT:TOK], SEL[0:NE, LAT:TOK], 0.0, ALU.add, ALU.max))
                V_.tensor_tensor(POS[0:NE], POS[0:NE], SEL[0:NE], ALU.mult).then_inc(MS_["aff"], 1)
                dve.wait_ge(MS_["pos_tr"], b["pos_tr"] + 1)
                V_.tensor_copy(POST, ps[:, 3, 0:NT * NE].rearrange("p (t e) -> p t e", t=NT)).then_inc(MS_["post"], 1)
                dve.wait_ge(MS_["post"], b["post"] + 1)

                def one_hot(out, pair):
                    return V_.tensor_tensor(out, SLOTNO[:].unsqueeze(1).unsqueeze(1).to_broadcast([P, NT, 2, CAP]),
                                            POST[:, :, bass.ds(2 * pair, 2)].unsqueeze(3).to_broadcast([P, NT, 2, CAP]), ALU.is_equal)

                def split_lo(base, place, lo, hi):
                    for i in range(lo, hi):
                        dve.wait_ge(MS_["hi"], b["hi"] + base + i + 1)
                        slot, at = (place + i) % SPLITS, i % 2 * PART
                        V_.tensor_tensor(W_LO[:, slot], RAW_W[:, (place + i) // 2 % RAWS, at:at + PART],
                                         W_HI[:, slot].bitcast(F32), ALU.subtract).then_inc(MS_["lo"], 1)

                def rest_of(out, src, hi):
                    return V_.tensor_tensor(out, src, hi.bitcast(F32), ALU.subtract)

                def hidden_lo(e):
                    for half in range(2):
                        dve.wait_ge(MS_["t_ev"], b["t_ev"] + 2 * e + half + 1)
                        rest_of(HTE_LO[:, 4 * half:4 * half + 4, :], ps[:, 6 + half, 0:4 * ROWS].rearrange("p (c r) -> p c r", c=4),
                                HTE_HI[:, 4 * half:4 * half + 4, :]).then_inc(MS_["t_lo"], 1)

                def expert_out_lo(e, odd):
                    dve.wait_ge(MS_["y_ev"], b["y_ev"] + e + 1)
                    at = 64 * odd
                    v = lambda y: y.rearrange("p (a n) -> p a n", a=2)
                    rest_of(v(YE_LO[at:at + CAP, 0, :]), ps[0:CAP, 4:6, :], v(YE_HI[at:at + CAP, 0, :]))
                    rest_of(v(YE_LO[at:at + CAPP, 1, :]), ps[CAP:ROWS, 4:6, :], v(YE_HI[at:at + CAPP, 1, :])).then_inc(MS_["y_lo"], 1)

                def combine_lo(pair):
                    dve.wait_ge(MS_["ct_ev"], b["ct_ev"] + 2 * (pair + 1))
                    rest_of(CT_LO[:, 0:4, :], ps[:, 6, :].rearrange("p (t n) -> p t n", t=4), CT_HI[:, 0:4, :]).then_inc(MS_["ct_lo"], 1)
                    rest_of(CT_LO[:, 4, :], ps[:, 7, 0:P], CT_HI[:, 4, :]).then_inc(MS_["ct_lo"], 1)

                def split_tokens(pair, odd):
                    dve.wait_ge(MS_["xh"], b["xh"] + 2 * pair + odd + 1)
                    rest_of(XET_LO[:, odd], XET[:, odd], XET_HI[:, odd]).then_inc(MS_["xl"], 1)

                def gather_rows(pair):
                    one_hot(OH, pair).then_inc(MS_["oh"], 1)

                def gated_rows(pair):
                    chain.link(one_hot(OH, pair))
                    V_.tensor_tensor(OH, OH, AFF[:, :, bass.ds(2 * pair, 2)].unsqueeze(3).to_broadcast([P, NT, 2, CAP]),
                                     ALU.mult).then_inc(MS_["ohg"], 1)

                def modulated(pair, step):
                    dve.wait_ge(MS_["x_mm"], b["x_mm"] + 3 * pair + step + 1)
                    u = step // 2
                    for k in ((0, 1, 2, 3), (4, 5, 6, 7), range(KD))[step]:
                        if u == 0:
                            src = ps[:, 6 + k // 4, k % 4 * P:(k % 4 + 1) * P].rearrange("p (e r) -> p e r", e=2)
                            dst = XET[:, :, k, 0:CAP]
                        else:
                            src = ps[:, 6, 2 * CAPP * k:2 * CAPP * (k + 1)].rearrange("p (e r) -> p e r", e=2)
                            dst = XET[:, :, k, CAP:ROWS]
                        last = V_.tensor_scalar(dst, src, scale_col(layer, 1, k, u), shift_col(layer, 1, k, u), ALU.mult, ALU.add)
                    last.then_inc(MS_["xt_ev"], 1)

                def hidden(e):
                    dve.wait_ge(MS_["sil"], b["sil"] + e + 1)
                    hid = HID[0:ROWS, :].rearrange("p (a n) -> p a n", a=2)
                    V_.tensor_tensor(hid, hid, ps[0:ROWS, 2:4, :], ALU.mult).then_inc(MS_["h"], 1)

                def accumulate(pair, tiles):
                    for t in tiles:
                        for half in range(2):
                            dve.wait_ge(MS_["c_mm"], b["c_mm"] + 10 * pair + 2 * t + half + 1)
                            dst = YB2[:, t, half * HALF:(half + 1) * HALF]
                            V_.tensor_tensor(dst, ps[:, 6 + half, :], dst, ALU.add).then_inc(MS_["c_ev"], 1)

                gather_rows(0)
                split_lo(0, 0, 0, 2)
                for step in range(3):
                    modulated(0, step)
                    if step < 2:
                        split_lo(0, 0, 2 + step, 3 + step)
                split_tokens(0, 0)
                split_lo(0, 0, 4, AHEAD)
                split_tokens(0, 1)
                dve.wait_ge(MS_["zero"], b["zero"] + 1)

                def turn(p, first, last):
                    base, place = first_part(p, first)
                    up_a, down_b, up_b, down_a = turn_parts(first)
                    at = AHEAD

                    def split_until(done):
                        nonlocal at
                        split_lo(base, place, at, done + AHEAD)
                        at = done + AHEAD

                    if not last:
                        gather_rows(p + 1)
                        for step in range(3):
                            split_until(4 * step + 5)
                            modulated(p + 1, step)
                    if not first:
                        split_until(up_a - 2)
                        gated_rows(p - 1)
                    split_until(up_a)
                    hidden(2 * p)
                    if not last:
                        split_until(up_a + 3)
                        split_tokens(p + 1, 0)
                    split_until(down_b + 4 * first)
                    hidden_lo(2 * p)
                    if not first:
                        expert_out_lo(2 * p - 1, 1)
                        split_until(down_b + 5)
                        combine_lo(p - 1)
                        for t in range(NT):
                            split_until(min(down_b + 9 + 2 * t, up_b))
                            accumulate(p - 1, (t,))
                    split_until(up_b)
                    hidden(2 * p + 1)
                    if not last:
                        split_until(up_b + 3)
                        split_tokens(p + 1, 1)
                    split_until(down_a)
                    hidden_lo(2 * p + 1)
                    expert_out_lo(2 * p, 0)

                turn(0, True, False)
                with dve.Fori(1, PAIRS - 1) as p:
                    chain.enter(p, 1, 1)
                    turn(p, False, False)
                chain.leave(PAIRS - 2)
                turn(PAIRS - 1, False, True)
                gated_rows(PAIRS - 1)
                split_lo(*first_part(PAIRS, False), AHEAD, 2 * DOWN)
                combine_lo(PAIRS - 1)
                gates_dve(n, layer, 1, HID.rearrange("p (j n) -> p j n", j=2))
                expert_out_lo(NE - 1, 1)
                accumulate(PAIRS - 1, range(NT))
                for t in range(NT + 2):
                    update(n, t, YB2)
                    if not layer:
                        normalise(n + 1, t - 2)
                dve.wait_ge(x_ready, NT * (n + 1))

            def rotate(x, cos, sin, ra, rb, dims):
                V_.tensor_tensor(ra, x, cos, ALU.mult)
                q = lambda v, i: v.rearrange("p g (b q r) -> p g b q r", b=2, q=2)[:, :, :, i]
                for i in range(2):
                    last = V_.tensor_tensor(q(rb, i), q(x, 1 - i), q(sin, i), ALU.mult)
                chain.link(last)
                return V_.tensor_tensor(x, ra, rb, ALU.add)

            def mla_dve():
                norm_dve(2, 1, 0)
                gates_dve(2, 1, 0, RAB)
                dve.wait_ge(cs_in, 16)
                dve.wait_ge(MA["ctx_in"], 64)
                dve.wait_ge(MA["lat_rstd"], 2)
                for t in range(NT):
                    for j, (lo, hi) in enumerate(((0, QL), (QL, QL + KVL))):
                        last = V_.tensor_scalar(LATN[:, t, lo:hi], LATN[:, t, lo:hi], LRS[:, j * NT + t:j * NT + t + 1], None, ALU.mult)
                    last.then_inc(MA["lat_n"], 1)
                dve.wait_ge(MA["lat_n"], NT)
                V_.tensor_tensor(CKO, LATN[:, NLAT, QL:QL + KVL], KVG, ALU.mult).then_inc(MA["cko"], 1)
                k = LATN[:, 0:NLAT, QL + KVL:WIN]
                ra = RA[:, 0:NLAT * ROPE].rearrange("p (t r) -> p t r", t=NLAT)
                rb = RB[:, 0:NLAT * ROPE].rearrange("p (t r) -> p t r", t=NLAT)
                dve.wait_ge(gate_mm, 12)
                chain.link(rotate(k, CS[:, 0], CS[:, 1], ra, rb, None))
                for j in range(2):
                    last = V_.tensor_copy(KRD[:, 1:NK, j * ROPE:(j + 1) * ROPE], LATN[:, :, QL + KVL:WIN])
                last.then_inc(MA["kr_ready"], 1)
                for t in range(NT):
                    dve.wait_ge(MA["ql_tr"], t + 1)
                    for c in range(3):
                        last = V_.tensor_scalar(QLT[:, c, t * P:(t + 1) * P], ps[:, 4 + t % 2, c * P:(c + 1) * P], NCOL[:, QN + c:QN + c + 1], None, ALU.mult)
                    last.then_inc(MA["ql_ev"], 1)
                for t in range(NLAT):
                    dve.wait_ge(MA["qr_ev"], t + 1)
                    if t >= 1:
                        dve.wait_ge(MA["qr_rot"], t)
                    v = lambda y: y.rearrange("p (h r) -> p h r", h=MH)
                    rotate(v(QR[:, t, :]), CS[:, 0, t, :].unsqueeze(1).to_broadcast([P, MH, ROPE]),
                           CS[:, 1, t, :].unsqueeze(1).to_broadcast([P, MH, ROPE]), v(RA), v(RB), None).then_inc(MA["qr_rot"], 1)

                def scores_max(h, t):
                    n = NT * h + t
                    dve.wait_ge(MA["s_mm"], n + 1)
                    b = (4, 6, 4, 6, 4)[t]
                    width = LAT + P if t < NLAT else P
                    src = ps[:, b:b + 2, :].rearrange("p a n -> p (a n)")[:, 0:width]
                    chain.link(V_.tensor_reduce(RMX[:, n % 2:n % 2 + 1], src, AX, ALU.max))
                    V_.tensor_scalar(RNM[:, n % 2:n % 2 + 1], RMX[:, n % 2:n % 2 + 1], -ATT_SCALE, None, ALU.mult).then_inc(MA["nm"], 1)

                def head_out(h):
                    dve.wait_ge(MA["o_mm"], 2 * h + 1)
                    V_.tensor_copy(OT[:, h, 0:LAT], ps[:, 2, :]).then_inc(MA["o_ev"], 1)
                    dve.wait_ge(MA["o_mm"], 2 * h + 2)
                    V_.tensor_copy(OT[:, h, LAT:TOK], ps[:, 3, 0:P]).then_inc(MA["o_ev"], 1)

                for h in range(MH):
                    scores_max(h, 0)
                    for t in range(NT):
                        if t + 1 < NT:
                            scores_max(h, t + 1)
                        n = NT * h + t
                        width = LAT + P if t < NLAT else P
                        dve.wait_ge(MA["e_done"], n + 1)
                        chain.link(V_.reciprocal(RRC[:, n % 2:n % 2 + 1], RSM[:, n % 2:n % 2 + 1]))
                        V_.tensor_scalar(PR[:, n % 2, 0:width], PR[:, n % 2, 0:width], RRC[:, n % 2:n % 2 + 1], None, ALU.mult).then_inc(MA["pr"], 1)
                        if t == 0 and h:
                            head_out(h - 1)
                head_out(MH - 1)
                for t in range(NT + 1):
                    update(2, t, B1)
                    normalise(3, t - 1)

            if STAGE >= 2:
                mix_dve(0)
            if STAGE >= 3:
                mla_dve()
                mix_dve(1)

        @block.tensor
        def _(pe):
            T = nc.tensor

            def mm(out, lhsT, rhs, first, last):
                return T.matmul(out, lhsT, rhs, start=first, stop=last)

            def tr(out, in_, n=P):
                return T.transpose(out, in_, IDENT[0:n, 0:n])

            pe.wait_ge(const_ready, 4)
            pe.wait_ge(rows_in, 16 * 8)
            tr(ps[:, 4, 0:COLS], RAW[0:COLS, 0, :], COLS).then_inc(cols_tr, 1)
            tr(ps[:, 5, 0:48], RAW[0:48, 1, :], 48).then_inc(cols_tr, 1)
            tr(ps[:, 6, 0:48], RAW[0:48, 2, :], 48).then_inc(cols_tr, 1)
            pe.wait_ge(cond_ready, 1)
            cond = NCOL[:, COND:QN].rearrange("p (c k) -> p c k", c=2)

            def ada_columns(n):
                pe.wait_ge(ada_ev, n + 1)
                if n >= 2:
                    pe.wait_ge(ada_col, n - 1)
                for q in range(4):
                    last = tr(ps[:, 2 + n % 2, 2 * q:2 * q + 2], AROW[0:2, n % 2, q * P:(q + 1) * P], 2)
                last.then_inc(ada_tr, 1)

            for n in range(ADA_FIRST):
                pe.wait_ge(w_in[2 + n], 16)
                if n >= 2:
                    pe.wait_ge(ada_ev, n - 1)
                for k in range(KD):
                    last = mm(ps[0:2, n % 2, :], cond[:, :, k], W8[:, 2 + n, k, :], k == 0, k == KD - 1)
                last.then_inc(ada_mm, 1)
                if n >= 1:
                    ada_columns(n - 1)
            ada_columns(ADA_FIRST - 1)

            def norm_pe(n):
                for t in range(NT):
                    pe.wait_ge(nt_xn, NT * n + t + 1)
                    if t >= 2:
                        pe.wait_ge(nt_evd, NT * n + t - 1)
                        pe.wait_ge(nt_eva, NT * n + t - 1)
                    for k in range(KD):
                        last = tr(ps[:, 4 + 2 * (t % 2) + k // 4, (k % 4) * P:(k % 4 + 1) * P], B1[:, t, k * P:(k + 1) * P])
                        if k % 4 == 3:
                            last.then_inc(nt_tr, 1)
                pe.wait_ge(nt_evd, NT * (n + 1))
                pe.wait_ge(nt_eva, NT * (n + 1))

            def gates_pe(n, diag, quarters=range(4)):
                for j in quarters:
                    pe.wait_ge(gate_diag, 4 * n + j + 1)
                    mm(ps[:, j, :], ONES[:], diag[:, j % 2, :], True, True).then_inc(gate_mm, 1)

            norm_pe(0)
            pe.wait_ge(cond_lo, 1)

            def ada_rows_ready(h, t):
                pe.wait_ge(ada2_ev, NT * h + t + 1)
                if t >= 2:
                    pe.wait_ge(ada2_col, NT * h + t - 1)

            def ada_columns2(t):
                for q in range(4):
                    last = tr(ps[:, 2 + t % 2, 4 * q:4 * q + 4], ROWS4[0:4, t % 2, q * P:(q + 1) * P], 4)
                last.then_inc(ada2_tr, 1)

            def ret_head(h, first):
                pe.wait_ge(w_in[0], 32 * (h + 1))
                if not first:
                    pe.wait_ge(st_ev, 4 * h)
                for u in range(4):
                    if u >= 2:
                        pe.wait_ge(qk_ev, 4 * h + u - 1)
                    b, w, m = 2 * (u % 2), u // 2, u % 2
                    for k in range(KD):
                        mm(ps[:, b, :], WQK[:, w, k, m * P:(m + 1) * P], HT[:, k, 0:LAT], k == 0, k == KD - 1)
                    for k in range(KD):
                        last = mm(ps[:, b + 1, 0:P], WQK[:, w, k, m * P:(m + 1) * P], HT[:, k, LAT:TOK], k == 0, k == KD - 1)
                    last.then_inc(qk_mm, 1)
                pe.wait_ge(w_in[1], 16 * (h + 1))
                if not first:
                    pe.wait_ge(yt_ev, NT * h)
                pe.wait_ge(qk_ev, 4 * (h + 1))
                if not first:
                    pe.wait_ge(out_acc, 2 * NT * h)
                for t in range(NT):
                    if t >= 2:
                        pe.wait_ge(v_ev, NT * h + t - 1)
                        pe.wait_ge(ada2_ev, NT * h + t - 1)
                    for k in range(KD):
                        if t and k == 4:
                            ada_rows_ready(h, t - 1)
                        value = mm(ps[:, 4 + t % 2, :], HT[:, k, t * P:(t + 1) * P], W8[:, 1, k, :], k == 0, k == KD - 1)
                        if k == KD - 1:
                            value.then_inc(v_mm, 1)
                        pe.wait_ge(ada2_lo, 40 * h + KD * t + k + 1)
                        mm(ps[0:4, 6 + t % 2, :], COND_HL[:, k, :], ADA_HI[:, k % 2], k == 0, False)
                        mm(ps[0:4, 6 + t % 2, :], COND_HL[:, k, :], ADA_LO[:, k % 2], False, k == KD - 1).then_inc(ada2_used, 1)
                        if t and k == 4:
                            ada_columns2(t - 1)
                pe.wait_ge(qk_ev, 4 * (h + 1))
                for t in range(NLAT):
                    if t == 1:
                        ada_rows_ready(h, NT - 1)
                    if t == 2:
                        ada_columns2(NT - 1)
                        pe.wait_ge(ada2_col, NT * (h + 1))
                    for m in range(2):
                        last = mm(ps[:, t, :], KT[:, m, t * P:(t + 1) * P], QT[:, m, 0:LAT], m == 0, m == 1)
                    last.then_inc(sc_mm, 1)
                for m in range(2):
                    last = mm(ps[:, 6, 0:P], KT[:, m, LAT:TOK], QT[:, m, LAT:TOK], m == 0, m == 1)
                last.then_inc(sc_mm, 1)
                for m in range(2):
                    last = tr(ps[:, 7, m * P:(m + 1) * P], KT[:, m, LAT:TOK])
                last.then_inc(kp_mm, 1)
                pe.wait_ge(w_in[2], 16 * (h + 2))
                pe.wait_ge(w_in[3], 16 * (h + 2))
                pe.wait_ge(s0_in, 32 * (h + 1))
                pe.wait_ge(v_ev, NT * (h + 1))
                pe.wait_ge(sc_ev, NT * (h + 1))
                for t in range(NT + 1):
                    if t < NT:
                        if t >= 2:
                            pe.wait_ge(yn_done, NT * h + t - 1)
                        if t < NLAT:
                            pe.wait_ge(qx_ready, NLAT * h + t + 1)
                            for j in range(NLAT):
                                mm(ps[:, t % 2, :], SC[:, j, t * P:(t + 1) * P], V[:, j, :], j == 0, False)
                            for j in range(4):
                                last = mm(ps[:, t % 2, :], QX[:, t % 2, j // 2, j % 2, :], S0[:, j // 2, j % 2, :], False, j == 3)
                        else:
                            last = mm(ps[:, t % 2, :], SCP, V[:, NLAT, :], True, True)
                        last.then_inc(y_mm, 1)
                    if t >= 1:
                        u = t - 1
                        pe.wait_ge(yn_done, NT * h + u + 1)
                        if u >= 2:
                            pe.wait_ge(yt_ev, NT * h + u - 1)
                        for c in range(4):
                            last = tr(ps[:, 4 + u % 2, c * P:(c + 1) * P], YN[:, u % 2, c * P:(c + 1) * P])
                        last.then_inc(yt_mm, 1)
                    if t < NT:
                        if t >= 2:
                            pe.wait_ge(silg, NT * h + t - 1)
                        for k in range(KD):
                            last = mm(ps[:, 2 + t % 2, :], HT[:, k, t * P:(t + 1) * P], W8[:, 2, k, :], k == 0, k == KD - 1)
                        last.then_inc(g_mm, 1)
                    if t >= 1:
                        pe.wait_ge(yt_ev, NT * h + u + 1)
                        if u == 0:
                            pe.wait_ge(kp_ev, h + 1)
                        else:
                            pe.wait_ge(out_acc, 2 * NT * h + 2 * u)
                        for half in range(2):
                            for c in range(4):
                                last = mm(ps[:, 6 + half, :], YT[:, u % 2, c, :], W4[:, 3, c, half * HALF:(half + 1) * HALF], c == 0, c == 3)
                            last.then_inc(out_mm, 1)
                pe.wait_ge(yn_done, NT * (h + 1))
                pe.wait_ge(silg, NT * (h + 1))
                for j in range(4):
                    mm(ps[:, j, :], KP[:, j // 2, (j % 2) * P:(j % 2 + 1) * P], V[:, NLAT, :], True, True).then_inc(st_mm, 1)

            ret_head(0, True)
            pe.wait_ge(st_ev, 4)
            gates_pe(0, ROWS4)
            pe.wait_ge(gate_ev, 4)
            with pe.Fori(1, HEADS) as h:
                ret_head(h, False)
            pe.wait_ge(out_acc, 2 * NT * HEADS)
            norm_pe(1)
            pe.wait_ge(st_ev, 4 * HEADS)

            def mix_pe(layer):
                b = {n: layer * v for n, v in per_layer.items()}
                pe.wait_ge(wr_in, 16 * (layer + 1))
                for k in range(KD):
                    mm(ps[0:NE, 0, :], WR[:, k, :], HT[:, k, 0:LAT], k == 0, k == KD - 1)
                for k in range(KD):
                    last = mm(ps[0:NE, 1, 0:P], WR[:, k, :], HT[:, k, LAT:TOK], k == 0, k == KD - 1)
                last.then_inc(MS_["lg_mm"], 1)
                pe.wait_ge(MS_["lt_ev"], b["lt_ev"] + 1)
                for t in range(NT):
                    last = tr(ps[:, 3, t * NE:(t + 1) * NE], SEL[0:NE, t * P:(t + 1) * P], NE)
                last.then_inc(MS_["lgt"], 1)
                pe.wait_ge(MS_["aff"], 2 * b["aff"] + 1)
                for t in range(NT):
                    last = tr(ps[0:NE, 1 + t // 4, (t % 4) * P:(t % 4 + 1) * P], AFF[:, t, :])
                last.then_inc(MS_["afft"], 1)
                pe.wait_ge(MS_["aff"], 2 * b["aff"] + 2)
                for t in range(NT):
                    last = tr(ps[:, 3, t * NE:(t + 1) * NE], POS[0:NE, t * P:(t + 1) * P], NE)
                last.then_inc(MS_["pos_tr"], 1)

                def gather(pair, step):
                    for k in ((0, 1, 2, 3), (4, 5, 6, 7), range(KD))[step]:
                        if step < 2:
                            for t in range(NLAT):
                                last = mm(ps[:, 6 + k // 4, k % 4 * P:(k % 4 + 1) * P], B1[:, t, k * P:(k + 1) * P],
                                          OH[:, t].rearrange("p e r -> p (e r)"), t == 0, t == NLAT - 1)
                        else:
                            last = mm(ps[:, 6, 2 * CAPP * k:2 * CAPP * (k + 1)], B1[:, NLAT, k * P:(k + 1) * P],
                                      OH[:, NLAT, :, 0:CAPP], True, True)
                    last.then_inc(MS_["x_mm"], 1)

                def part(n, place, out, tokens, k):
                    pe.wait_ge(MS_["lo"], b["lo"] + n + 1)
                    slot = place % SPLITS
                    for i, (x, w) in enumerate(((0, W_HI), (0, W_LO), (1, W_HI))):
                        for half in range(2):
                            last = mm(ps[0:ROWS, out + half, :], tokens[x][:, k, :], w[:, slot, half * HALF:(half + 1) * HALF],
                                      k == 0 and i == 0, k == KD - 1 and i == 2)
                    last.then_inc(MS_["used"], 1)

                def up(n, place, par, lo, hi):
                    tokens = (XET_HI[:, par], XET_LO[:, par])
                    for i in range(lo, hi):
                        part(n + i, place + i, 2 * (i // 2 % 2), tokens, i // 4 * 2 + i % 2)

                def down(n, place, lo, hi):
                    for i in range(lo, hi):
                        part(n + i, place + i, 4, (HTE_HI[:], HTE_LO[:]), i)

                def hidden_tr(e):
                    pe.wait_ge(MS_["h"], b["h"] + e + 1)
                    for c in range(KD):
                        last = tr(ps[:, 6 + c // 4, (c % 4) * ROWS:(c % 4 + 1) * ROWS], HID[0:ROWS, c * P:(c + 1) * P], ROWS)
                        if c % 4 == 3:
                            last.then_inc(MS_["t_mm"], 1)

                def combine_tr(pair):
                    pe.wait_ge(MS_["ohg"], b["ohg"] + pair + 1)
                    for t in range(NT):
                        last = tr(ps[:, 6 + t // 4, (t % 4) * P:(t % 4 + 1) * P], OH[:, t].rearrange("p e r -> p (e r)"))
                        if t >= 3:
                            last.then_inc(MS_["ct_mm"], 1)

                def combine(pair, tiles):
                    if tiles[0] == 0:
                        pe.wait_ge(MS_["ct_lo"], b["ct_lo"] + 2 * (pair + 1))
                        pe.wait_ge(MS_["y_lo"], b["y_lo"] + 2 * (pair + 1))
                    for t in tiles:
                        for half in range(2):
                            if t >= 1:
                                pe.wait_ge(MS_["c_ev"], b["c_ev"] + 10 * pair + 2 * t + half - 1)
                            for i, (c, y) in enumerate(((CT_HI, YE_HI), (CT_HI, YE_LO), (CT_LO, YE_HI))):
                                last = mm(ps[:, 6 + half, :], c[:, t, :], y[:, t // NLAT, half * HALF:(half + 1) * HALF], i == 0, i == 2)
                            last.then_inc(MS_["c_mm"], 1)

                pe.wait_ge(MS_["oh"], b["oh"] + 1)
                gather(0, 0)
                gather(0, 1)
                pe.wait_ge(MS_["xt_ev"], b["xt_ev"] + 1)
                gather(0, 2)

                def turn(p, first, last):
                    base, place = first_part(p, first)
                    up_a, down_b, up_b, down_a = turn_parts(first)
                    if not first:
                        pe.wait_ge(MS_["h"], b["h"] + 2 * p)
                    pe.wait_ge(MS_["xl"], b["xl"] + 2 * p + 1)
                    for step in range(4):
                        up(base, place, 0, 4 * step, 4 * step + 4)
                        if not last and step < 3:
                            if step == 0:
                                pe.wait_ge(MS_["oh"], b["oh"] + p + 2)
                                if not first:
                                    pe.wait_ge(MS_["t_lo"], b["t_lo"] + 4 * p)
                            if step == 2:
                                pe.wait_ge(MS_["xt_ev"], b["xt_ev"] + 3 * (p + 1) + 1)
                            gather(p + 1, step)
                    if not first:
                        pe.wait_ge(MS_["t_lo"], b["t_lo"] + 4 * p)
                        pe.wait_ge(MS_["y_lo"], b["y_lo"] + 2 * p - 1)
                        down(base + up_a, place + up_a, 0, 4)
                        if not last:
                            pe.wait_ge(MS_["xt_ev"], b["xt_ev"] + 3 * (p + 2))
                        hidden_tr(2 * p)
                        down(base + up_a, place + up_a, 4, 2 * DOWN)
                    pe.wait_ge(MS_["h"], b["h"] + 2 * p + 1)
                    pe.wait_ge(MS_["xl"], b["xl"] + 2 * p + 2)
                    up(base + down_b, place + down_b, 1, 0, 4)
                    if first:
                        pe.wait_ge(MS_["xt_ev"], b["xt_ev"] + 3 * (p + 2))
                        hidden_tr(2 * p)
                        up(base + down_b, place + down_b, 1, 4, 16)
                    else:
                        pe.wait_ge(MS_["t_lo"], b["t_lo"] + 4 * p + 2)
                        up(base + down_b, place + down_b, 1, 4, 5)
                        combine_tr(p - 1)
                        up(base + down_b, place + down_b, 1, 5, 8)
                        for t in range(NT):
                            combine(p - 1, (t,))
                            up(base + down_b, place + down_b, 1, 8 + 2 * t, min(10 + 2 * t, 2 * UP))
                    pe.wait_ge(MS_["t_lo"], b["t_lo"] + 4 * p + 2)
                    if not first:
                        pe.wait_ge(MS_["y_lo"], b["y_lo"] + 2 * p)
                    down(base + up_b, place + up_b, 0, 4)
                    if not first:
                        pe.wait_ge(MS_["c_ev"], b["c_ev"] + 10 * p)
                    hidden_tr(2 * p + 1)
                    down(base + up_b, place + up_b, 4, 2 * DOWN)

                turn(0, True, False)
                with pe.Fori(1, PAIRS - 1) as p:
                    turn(p, False, False)
                turn(PAIRS - 1, False, True)
                base, place = first_part(PAIRS, False)
                pe.wait_ge(MS_["t_lo"], b["t_lo"] + 2 * NE)
                pe.wait_ge(MS_["y_lo"], b["y_lo"] + NE - 1)
                down(base, place, 0, 4)
                combine_tr(PAIRS - 1)
                for j in range(4):
                    down(base, place, 4 + j, 5 + j)
                    gates_pe(2 * layer + 1, HID.rearrange("p (j n) -> p j n", j=2), (j,))
                combine(PAIRS - 1, range(NT))

            def mla_pe():
                pe.wait_ge(gate_ev, 8)
                norm_pe(2)
                base = [16 * n for n in BEFORE_MLA]
                for s in range(2):
                    pe.wait_ge(w_in[s], base[s] + 16)
                for t in range(NT):
                    if t >= 2:
                        pe.wait_ge(MA["lat_ev"], t - 1)
                    b = 2 * (t % 2)
                    for n, (lo, hi) in enumerate(((0, HALF), (HALF, WIN))):
                        for k in range(KD):
                            last = mm(ps[:, b + n, 0:hi - lo], HT[:, k, t * P:(t + 1) * P], WIN2[k // 4][:, k % 4, lo:hi], k == 0, k == KD - 1)
                    last.then_inc(MA["lat_mm"], 1)
                pe.wait_ge(MA["lat_ev"], NT)
                gates_pe(2, RAB)
                for t in range(NT):
                    pe.wait_ge(MA["lat_n"], t + 1)
                    if t >= 2:
                        pe.wait_ge(MA["ql_ev"], t - 1)
                    for c in range(3):
                        last = tr(ps[:, 4 + t % 2, c * P:(c + 1) * P], LATN[:, t, c * P:(c + 1) * P])
                    last.then_inc(MA["ql_tr"], 1)
                pe.wait_ge(MA["kr_ready"], 1)
                for kt in range(NK):
                    if kt >= 2:
                        pe.wait_ge(MA["kv_ev"], kt - 1)
                    for c in range(2):
                        src = CKC[:, c * P:(c + 1) * P] if kt == 0 else LATN[:, kt - 1, QL + c * P:QL + (c + 1) * P]
                        tr(ps[:, 6 + kt % 2, c * P:(c + 1) * P], src)
                    tr(ps[:, 6 + kt % 2, 2 * P:3 * P], KRD[:, kt, :]).then_inc(MA["kv_tr"], 1)
                pe.wait_ge(MA["ql_ev"], NT)
                pe.wait_ge(gate_ev, 12)
                for s in (2, 3):
                    pe.wait_ge(w_in[s], base[s] + 16)
                for t in range(NT):
                    if t == 4:
                        pe.wait_ge(MA["qr_ev"], 1)
                    for g in range(2):
                        for c in range(3):
                            last = mm(ps[:, t % 4, g * 256:(g + 1) * 256], QLT[:, c, t * P:(t + 1) * P], WQB[g][:, c, :, P:P + ROPE], c == 0, c == 2)
                    last.then_inc(MA["qr_mm"], 1)
                pe.wait_ge(w_in[0], base[0] + 32)
                pe.wait_ge(MA["kv_ev"], NK)
                for kt in range(NK):
                    for half in range(2):
                        if kt >= 1:
                            pe.wait_ge(MA["vv_ev"], 2 * kt + half - 1)
                        for c in range(2):
                            last = mm(ps[:, 6 + half, :], KVT[:, c, kt * P:(kt + 1) * P], WKV[:, c, 4 * half:4 * half + 4, P:2 * P], c == 0, c == 1)
                        last.then_inc(MA["vv_mm"], 1)
                for t in range(NT):
                    pe.wait_ge(*((MA["qr_rot"], t + 1) if t < NLAT else (MA["qr_ev"], NT)))
                    if t >= 2:
                        pe.wait_ge(MA["qrt_ev"], t - 1)
                    for c in range(4):
                        last = tr(ps[:, 4 + t % 2, c * P:(c + 1) * P], QR[:, t, c * P:(c + 1) * P])
                    last.then_inc(MA["qrt_tr"], 1)
                pe.wait_ge(MA["qrt_ev"], NT)
                pe.wait_ge(MA["vv_ev"], 2 * NK)

                def scores(h, t):
                    n = NT * h + t
                    if t >= 2:
                        pe.wait_ge(MA["e_done"], n - 1)
                    elif h:
                        pe.wait_ge(MA["e_done"], NT * h)
                    b = (4, 6, 4, 6, 4)[t]
                    r = ROPE * (h % 2)
                    for lo, hi in (((0, HALF), (HALF, LAT + P)) if t < NLAT else ((LAT + P, NK * P),)):
                        mm(ps[:, b, 0:hi - lo], QNT[:, h % 2, t * P:(t + 1) * P], KNT[:, h % 2, lo:hi], True, False)
                        last = mm(ps[:, b, 0:hi - lo], QRT[r:r + ROPE, h // 2, t * P:(t + 1) * P], KRT[r:r + ROPE, lo:hi], False, True)
                        b += 1
                    last.then_inc(MA["s_mm"], 1)

                def project_keys(h):
                    for n, (lo, hi) in enumerate(((0, HALF), (HALF, NK * P))):
                        for c in range(2):
                            last = mm(ps[:, 2 + n, 0:hi - lo], WKV[:, c, h, 0:P], KVT[:, c, lo:hi], c == 0, c == 1)
                    last.then_inc(MA["kn_mm"], 1)

                def project_queries(h):
                    pe.wait_ge(MA["kn_ev"], 2 * h + 1)
                    for n, (lo, hi) in enumerate(((0, HALF), (HALF, TOK))):
                        for c in range(3):
                            last = mm(ps[:, 2 + n, 0:hi - lo], WQB[h // 4][:, c, h % 4, 0:P], QLT[:, c, lo:hi], c == 0, c == 2)
                    last.then_inc(MA["kn_mm"], 1)

                def head_out(h):
                    pe.wait_ge(MA["pt_ev"], NT * (h + 1))
                    for kt in range(NT):
                        last = mm(ps[:, 2, :], B1[:, kt, h * P:(h + 1) * P], PT[:, kt, :], kt == 0, kt == NT - 1)
                    last.then_inc(MA["o_mm"], 1)
                    mm(ps[:, 3, 0:P], VP[:, h * P:(h + 1) * P], PTP, True, True).then_inc(MA["o_mm"], 1)

                project_keys(0)
                project_queries(0)
                for h in range(MH):
                    pe.wait_ge(MA["kn_ev"], 2 * (h + 1))
                    scores(h, 0)
                    for t in range(NT):
                        if t + 1 < NT:
                            scores(h, t + 1)
                        if t == 0 and h:
                            head_out(h - 1)
                        if t == 1 and h + 1 < MH:
                            pe.wait_ge(MA["o_ev"], 2 * h) if h else None
                            project_keys(h + 1)
                        if t == 2 and h + 1 < MH:
                            project_queries(h + 1)
                        n = NT * h + t
                        pe.wait_ge(MA["pr"], n + 1)
                        if n:
                            pe.wait_ge(MA["pt_ev"], n)
                        for kt in range(NT if t < NLAT else 1):
                            last = tr(ps[:, kt // 4, (kt % 4) * P:(kt % 4 + 1) * P], PR[:, n % 2, kt * P:(kt + 1) * P])
                        last.then_inc(MA["pt_tr"], 1)
                head_out(MH - 1)
                pe.wait_ge(w_in[1], base[1] + 32)
                pe.wait_ge(w_in[2], base[2] + 32)
                pe.wait_ge(MA["o_ev"], 2 * MH)
                for t in range(NT):
                    for half in range(2):
                        if t >= 2:
                            pe.wait_ge(MA["mo_ev"], 2 * (t - 2) + half + 1)
                        for k in range(MH):
                            last = mm(ps[:, 4 + 2 * (t % 2) + half, :], OT[:, k, t * P:(t + 1) * P], W4[:, 1 + k // 4, k % 4, half * HALF:(half + 1) * HALF],
                                      k == 0, k == MH - 1)
                        last.then_inc(MA["mo_mm"], 1)
                pe.wait_ge(MA["mo_ev"], 2 * NT)
                norm_pe(3)

            if STAGE >= 2:
                mix_pe(0)
            if STAGE >= 3:
                mla_pe()
                mix_pe(1)


_INS = ["x_prompt", "x_sample", "state_ret_fwd", "state_ret_bwd", "cache_mla_ckv", "cache_mla_krope", "c", "c_ctx",
        "ada_w", "ada_b", "norm_pre", "norm_post", "ret_w_in", "ret_decay_fwd", "ret_decay_bwd", "ret_w_out",
        "mla_w_in", "mla_q_norm", "mla_kv_norm", "mla_w_q_b", "mla_w_kv_b", "mla_w_out",
        "moe_w_router", "moe_w_gate", "moe_w_up", "moe_w_down"]
_OUTS = [("y_prompt", (1, 128, 1024)), ("y_sample", (1, 512, 1024)), ("state_fwd", (1, 1, 4, 256, 512)),
         ("state_bwd", (1, 1, 4, 256, 512)), ("new_ckv", (1, 1, 128, 256)), ("new_krope", (1, 1, 128, 64))]


def rotary_tables():
    import numpy as np
    grid, half = 64, ROPE // 2
    row = np.repeat(np.arange(LAT // grid, dtype=np.float32), grid)
    col = np.tile(np.arange(grid, dtype=np.float32), LAT // grid)
    inv = (np.float32(1.0) / (np.float32(10000.0) ** (np.arange(0, half, 2, dtype=np.float32) / np.float32(half)))).astype(np.float32)
    ar, ac = row[:, None] * inv, col[:, None] * inv
    ang = np.concatenate([ar, ar, ac, ac], axis=-1).astype(np.float32)
    sign = np.repeat(np.array([-1, 1, -1, 1], np.float32), half // 2)
    return np.stack([np.cos(ang), np.sin(ang) * sign]).astype(np.float32)


STAGE = 3


def kernel(**inputs):
    import numpy as _np
    import concourse.bacc as _bacc
    from concourse import mybir as _mybir
    from concourse.bass_utils import run_bass_kernel_spmd as _run

    nc = _bacc.Bacc("TRN2", target_bir_lowering=False, num_devices=1)
    arrays, a, o = {}, {}, {}
    for name in _INS + ["rotary"]:
        x = rotary_tables() if name == "rotary" else _np.ascontiguousarray(inputs[name])
        arrays[f"in_{name}_dram"] = x
        a[name] = nc.dram_tensor(f"in_{name}_dram", x.shape, _mybir.dt.from_np(x.dtype), kind="ExternalInput").ap()
    for name, shape in _OUTS:
        o[name] = nc.dram_tensor(f"out_{name}_dram", shape, _mybir.dt.float32, kind="ExternalOutput").ap()
    trunk(nc, a, o, STAGE)
    r = _run(nc, [arrays], core_ids=[0])
    return tuple(r.results[0][f"out_{name}_dram"] for name, _ in _OUTS)
```
